# Optimizing a Trainium2 kernel written in Bass

```python
import jax, jax.numpy as jnp
from jax import lax
import numpy as np

D_MODEL = 2048
BATCH = 1
SEQ = 1024
DEPTH = 1

CHUNK = 64
N_META = 16
D_MIX = D_MODEL
POOL_WIDTH = D_MIX // 2
POOL_WINDOWS = (2, 4, 8, 16)
POOL_GROUP = POOL_WIDTH // len(POOL_WINDOWS)
ATTN_WIDTH = D_MIX - POOL_WIDTH
HEAD_DIM = 64
N_Q_HEADS = ATTN_WIDTH // HEAD_DIM
N_KV_HEADS = max(1, N_Q_HEADS // 8)
GQA_GROUP = N_Q_HEADS // N_KV_HEADS
KV_WIDTH = N_KV_HEADS * HEAD_DIM
WINDOW = 128
WINDOW_CHUNKS = WINDOW // CHUNK
EPS = 1e-6
NEG_INF = -1e30
IN_COLS = 2 * POOL_WIDTH + ATTN_WIDTH + 2 * KV_WIDTH + ATTN_WIDTH
SPLITS = [POOL_WIDTH,
          2 * POOL_WIDTH,
          2 * POOL_WIDTH + ATTN_WIDTH,
          2 * POOL_WIDTH + ATTN_WIDTH + KV_WIDTH,
          2 * POOL_WIDTH + ATTN_WIDTH + 2 * KV_WIDTH]

kernel_name = "hymba_pool_swa_sink_hybrid"

def _rmsnorm(x, g):
    xf = x.astype(jnp.float32)
    y = xf * lax.rsqrt(jnp.mean(xf * xf, axis=-1, keepdims=True) + EPS)
    return (y * g.astype(jnp.float32)).astype(x.dtype)

def _multiscale_pool(v, pool_w, pool_scale):
    b, l, c = v.shape
    vf = v.astype(jnp.float32)
    cs = jnp.cumsum(vf, axis=1)
    t = jnp.arange(l)
    outs = []
    for gi, w in enumerate(POOL_WINDOWS):
        sl = slice(gi * POOL_GROUP, (gi + 1) * POOL_GROUP)
        cg = cs[..., sl]
        lower = jnp.pad(cg, ((0, 0), (w, 0), (0, 0)))[:, :l]
        cnt = jnp.minimum(t + 1, w).astype(jnp.float32)[None, :, None]
        outs.append((cg - lower) / cnt - vf[..., sl])
    d = jnp.stack(outs, axis=2)
    mixed = jnp.einsum('blgc,gcd->blgd', d, pool_w.astype(jnp.float32))
    return (mixed.reshape(b, l, c) * pool_scale.astype(jnp.float32)).astype(v.dtype)

def _gqa_sink_attend(q, k, v, mask, sinks):
    s = jnp.einsum('bcqhgd,bckhd->bchgqk', q.astype(jnp.float32),
                   k.astype(jnp.float32)) * (HEAD_DIM ** -0.5)
    s = jnp.where(mask[None, :, None, None, None, :], s, NEG_INF)
    sink = jnp.broadcast_to(sinks.astype(jnp.float32)[None, None, :, :, None, None],
                            s.shape[:-1] + (1,))
    p = jax.nn.softmax(jnp.concatenate([s, sink], axis=-1), axis=-1)[..., :-1]
    o = jnp.einsum('bchgqk,bckhd->bcqhgd', p, v.astype(jnp.float32))
    return o.astype(q.dtype)

def _attention_branch(q, k, v, q_norm_g, k_norm_g, sinks):
    b, l, _ = q.shape
    s_len = l - N_META
    n_chunks = s_len // CHUNK
    q = _rmsnorm(q.reshape(b, l, N_KV_HEADS, GQA_GROUP, HEAD_DIM), q_norm_g)
    k = _rmsnorm(k.reshape(b, l, N_KV_HEADS, HEAD_DIM), k_norm_g)
    v = v.reshape(b, l, N_KV_HEADS, HEAD_DIM)
    sk = sinks.reshape(N_KV_HEADS, GQA_GROUP)

    o_meta = _gqa_sink_attend(q[:, None, :N_META], k[:, None, :N_META], v[:, None, :N_META],
                              jnp.ones((1, N_META), dtype=bool), sk)

    qc = q[:, N_META:].reshape(b, n_chunks, CHUNK, N_KV_HEADS, GQA_GROUP, HEAD_DIM)

    def band(t):
        meta = jnp.broadcast_to(t[:, None, :N_META], (b, n_chunks, N_META) + t.shape[2:])
        chunks = t[:, N_META:].reshape(b, n_chunks, CHUNK, N_KV_HEADS, HEAD_DIM)
        parts = [meta]
        for off in range(WINDOW_CHUNKS - 1, 0, -1):
            parts.append(jnp.pad(chunks, ((0, 0), (off, 0), (0, 0), (0, 0), (0, 0)))[:, :n_chunks])
        parts.append(chunks)
        return jnp.concatenate(parts, axis=2)

    cidx = jnp.arange(n_chunks)[:, None]
    mask_parts = [jnp.ones((n_chunks, N_META), dtype=bool)]
    for off in range(WINDOW_CHUNKS - 1, 0, -1):
        mask_parts.append(jnp.broadcast_to(cidx >= off, (n_chunks, CHUNK)))
    mask_parts.append(jnp.ones((n_chunks, CHUNK), dtype=bool))
    mask = jnp.concatenate(mask_parts, axis=1)

    o_real = _gqa_sink_attend(qc, band(k), band(v), mask, sk)
    return jnp.concatenate([o_meta.reshape(b, N_META, ATTN_WIDTH),
                            o_real.reshape(b, s_len, ATTN_WIDTH)], axis=1)

def setup_inputs(seed: int = 0) -> dict:
    key = jax.random.key(seed)
    ks = jax.random.split(key, 10)
    f32 = jnp.float32
    x = jax.random.normal(ks[0], (BATCH, SEQ, D_MODEL), f32)
    meta_tokens = jax.random.normal(ks[1], (N_META, D_MODEL), f32)
    norm_g = 1.0 + 0.02 * jax.random.normal(ks[2], (DEPTH, D_MODEL), f32)
    w_in = jax.random.normal(ks[3], (DEPTH, D_MODEL, IN_COLS), f32) * D_MODEL ** -0.5
    pool_w = jax.random.normal(ks[4], (DEPTH, len(POOL_WINDOWS), POOL_GROUP, POOL_GROUP), f32) * POOL_GROUP ** -0.5
    pool_scale = 1.0 + 0.02 * jax.random.normal(ks[5], (DEPTH, POOL_WIDTH), f32)
    q_norm_g = 1.0 + 0.02 * jax.random.normal(ks[6], (DEPTH, HEAD_DIM), f32)
    k_norm_g = 1.0 + 0.02 * jax.random.normal(ks[7], (DEPTH, HEAD_DIM), f32)
    sinks = 0.5 * jax.random.normal(ks[8], (DEPTH, N_Q_HEADS), f32)
    w_out = jax.random.normal(ks[9], (DEPTH, D_MIX, D_MODEL), f32) * D_MIX ** -0.5
    return {"x": x, "meta_tokens": meta_tokens, "norm_g": norm_g, "w_in": w_in,
            "pool_w": pool_w, "pool_scale": pool_scale, "q_norm_g": q_norm_g,
            "k_norm_g": k_norm_g, "sinks": sinks, "w_out": w_out}

def reference(x, meta_tokens, norm_g, w_in, pool_w, pool_scale, q_norm_g, k_norm_g, sinks, w_out):
    b, _, d = x.shape
    meta = jnp.broadcast_to(meta_tokens[None].astype(x.dtype), (b, N_META, d))
    h = jnp.concatenate([meta, x], axis=1)
    for layer in range(DEPTH):
        hn = _rmsnorm(h, norm_g[layer])
        proj = hn @ w_in[layer]
        pv, pg, q, k, v, ag = jnp.split(proj, SPLITS, axis=-1)
        pool_out = _multiscale_pool(pv, pool_w[layer], pool_scale[layer])
        attn_out = _attention_branch(q, k, v, q_norm_g[layer], k_norm_g[layer], sinks[layer])
        mixed = jnp.concatenate([jax.nn.silu(pg) * pool_out,
                                 jax.nn.silu(ag) * attn_out], axis=-1)
        h = h + mixed @ w_out[layer]
    return h[:, N_META:]


_drawn_inputs = setup_inputs


def setup_inputs(seed=0):
    import zlib

    import numpy as np

    out = dict(_drawn_inputs(seed))
    spreads = {}
    factors = {'meta_tokens': 2.816,
     'norm_g': 5.44,
     'pool_scale': 7.857,
     'q_norm_g': 8.0,
     'k_norm_g': 8.0,
     'sinks': 8.0}
    for name, (base, spread) in spreads.items():
        noise = np.random.default_rng([zlib.crc32(name.encode()), seed]).standard_normal(out[name].shape)
        drawn = base * np.exp(spread * noise) if base else spread * noise
        out[name] = __import__('jax').numpy.asarray(drawn.astype(out[name].dtype))
    for name, factor in factors.items():
        out[name] = (out[name] * factor).astype(out[name].dtype)
    return out
```

```python
from contextlib import ExitStack

import concourse.bass as bass
from concourse import mybir

P = 128
D = 2048
KT = D // P
META = 16
SEQ = 1024
HALF = 512
HALVES = SEQ // HALF
COLS = META + HALF
SUB = COLS // 2
CHUNK = 64
NCH = HALF // CHUNK
HD = 64
PAIRS = 8
KVH = 2
GROUPS = 4
QUAD = 4
BAND = META + CHUNK
KEYS = BAND + CHUNK
EPS = 1e-6
MASKED = -1e30
ONE = 1

BLK = 512
TILE_BLKS = 4
RAW = 4
SPLIT = 4
LEAD = 3
KV_BLKS = 2 * TILE_BLKS
Q_BLKS = PAIRS * TILE_BLKS
G_BLKS = 6 * TILE_BLKS
IN_BLKS = KV_BLKS + Q_BLKS + GROUPS * G_BLKS
OB = D // BLK
OUT_BLKS = OB * KT
NBLK = IN_BLKS + OUT_BLKS
ROWT = HALF // P
XT = 1 + ROWT
XG = 1 + 4 * ROWT
UNITS = 4

C_ID, C_BLK, C_ONE, C_MASK = 0, 128, 256, 384
C_INVW = C_MASK + HALVES * KEYS
C_EPS = C_INVW + GROUPS
C_N = C_EPS + 1
V_SCALE, V_SINK, V_GQ, V_GK = 0, 8, 16, 17
V_N = 18


def hymba_layer(nc, xcat, norm_g, w_in, w_out, pool_w, vecs, consts, out):
    f32, f32r, bf16 = mybir.dt.float32, mybir.dt.float32r, mybir.dt.bfloat16
    ACT = mybir.ActivationFunctionType
    ALU = mybir.AluOpType
    AX = mybir.AxisListType

    ctx = ExitStack()
    with ctx:
        def sb(name, shape, dt=f32):
            return ctx.enter_context(nc.sbuf_tensor(name, shape, dt))

        def sem(name):
            return ctx.enter_context(nc.semaphore(name))

        act_h = sb("act_h", [P, KT, COLS], f32r)
        act_l = sb("act_l", [P, KT, COLS], f32r)
        mixed = sb("mixed", [P, KT, HALF])
        raw = sb("raw", [P, RAW, BLK])
        wh = sb("wh", [P, SPLIT, BLK], f32r)
        wl = sb("wl", [P, SPLIT, BLK], f32r)
        kT = sb("kT", [P, CHUNK + HALF])
        vT = sb("vT", [P, CHUNK + HALF])
        k_meta = sb("k_meta", [P, HALVES, META])
        v_meta = sb("v_meta", [P, HALVES, META])
        cst = sb("cst", [P, C_N])
        vec = sb("vec", [P, V_N])
        gq8 = sb("gq8", [P, 1])
        xss = sb("xss", [P, XT])
        xsd = sb("xsd", [P, XT])
        xrs = sb("xrs", [P, XT])
        kb_h = sb("kb_h", [P, KVH, (NCH + 1) * BAND], f32r)
        kb_l = sb("kb_l", [P, KVH, (NCH + 1) * BAND], f32r)
        v_h = sb("v_h", [P, NCH, 2, HD], f32r)
        v_l = sb("v_l", [P, NCH, 2, HD], f32r)
        vm_h = sb("vm_h", [META, 2, HD], f32r)
        vm_l = sb("vm_l", [META, 2, HD], f32r)
        qd_h = sb("qd_h", [P, QUAD, 2, CHUNK], f32r)
        qd_l = sb("qd_l", [P, QUAD, 2, CHUNK], f32r)
        pt_h = sb("pt_h", [P, QUAD * P], f32r)
        pt_l = sb("pt_l", [P, QUAD * P], f32r)
        pm_h = sb("pm_h", [META, QUAD * P], f32r)
        pm_l = sb("pm_l", [META, QUAD * P], f32r)
        d_h = sb("d_h", [P, 2, HALF], f32r)
        d_l = sb("d_l", [P, 2, HALF], f32r)
        pw_h = sb("pw_h", [P, BLK], f32r)
        pw_l = sb("pw_l", [P, BLK], f32r)
        smax = sb("smax", [P, QUAD])
        nmax = sb("nmax", [P, QUAD])
        den = sb("den", [P, QUAD])
        esink = sb("esink", [P, QUAD])
        dtot = sb("dtot", [P, QUAD])
        rden = sb("rden", [P, QUAD])

        scr = sb("scr", [P, 7168])
        x_t = [scr[:, 0:D], scr[:, D:2 * D]]
        g_row = scr[:, 2 * D:3 * D]
        junk = scr[:, 3 * D:3 * D + D // 2].bitcast(bf16)
        k_dup = scr[:, 0:1184].rearrange("p (h c) -> p h c", h=KVH)
        k_sq, k_rs = scr[:, 1184:1712], scr[:, 1712:2240]
        q_sq = [scr[:, 2240:2752], scr[:, 2752:3264]]
        q_rs = [scr[:, 3264:3776], scr[:, 3776:4288]]
        prob = scr[:, 0:QUAD * KEYS].rearrange("p (c k) -> p c k", c=QUAD)
        pn = scr[:, 576:1088]
        pnm = scr[:, 1088:1152]
        gate = [scr[:, 1152 + HALF * n:1152 + HALF * (n + 1)] for n in range(4)]
        pv = [scr[:, 3200:3728], scr[:, 3728:4256]]
        v_all = scr[:, 4288:5312].rearrange("p (c n) -> p c n", c=NCH)
        psum_w = [scr[:, 5312:5840], scr[:, 5840:6368]]
        pw_raw = scr[:, 6368:6880]
        vm_all = scr[0:META, 6880:7008]

        R = [ctx.enter_context(nc.psum_tensor(f"R{i}", [P, BLK], f32)) for i in range(3)]
        S = ctx.enter_context(nc.psum_tensor("S", [P, 2, BLK], f32))
        PT = ctx.enter_context(nc.psum_tensor("PT", [P, BLK], f32))
        PM = ctx.enter_context(nc.psum_tensor("PM", [P, BLK], f32))
        O = ctx.enter_context(nc.psum_tensor("O", [P, BLK], f32))
        XB = [R[0], R[1], R[2], O]

        ident = cst[:, C_ID:C_ID + P]
        blkones = cst[:, C_BLK:C_BLK + P]
        ones_row = cst[0:1, C_ONE:C_ONE + P]

        s_cst = sem("s_cst")
        s_g = sem("s_g")
        s_x = [sem(f"s_x{i}") for i in range(2)]
        s_raw = [sem(f"s_raw{i}") for i in range(RAW)]
        s_pw = sem("s_pw")
        s_res = [sem(f"s_res{i}") for i in range(ROWT)]
        s_out = [sem(f"s_out{i}") for i in range(ROWT)]
        s_free = sem("s_free")
        s_init = sem("s_init")
        s_gq = sem("s_gq")
        s_wh = sem("s_wh")
        s_wl = sem("s_wl")
        s_blk = sem("s_blk")
        s_xsq = sem("s_xsq")
        s_xsd = sem("s_xsd")
        s_xrs = sem("s_xrs")
        s_xn = sem("s_xn")
        s_xt = sem("s_xt")
        s_xh = sem("s_xh")
        s_xl = sem("s_xl")
        s_ksq = sem("s_ksq")
        s_kss = sem("s_kss")
        s_ksd = sem("s_ksd")
        s_krs = sem("s_krs")
        s_kn = sem("s_kn")
        s_kd = sem("s_kd")
        s_kbh = sem("s_kbh")
        s_kbl = sem("s_kbl")
        s_vT = sem("s_vT")
        s_vt = sem("s_vt")
        s_va = sem("s_va")
        s_vh = sem("s_vh")
        s_vl = sem("s_vl")
        s_qsq = sem("s_qsq")
        s_qss = sem("s_qss")
        s_qsd = sem("s_qsd")
        s_qrs = sem("s_qrs")
        s_qn = sem("s_qn")
        s_qdh = sem("s_qdh")
        s_qdl = sem("s_qdl")
        s_s = sem("s_s")
        s_mx = sem("s_mx")
        s_nm = sem("s_nm")
        s_ex = sem("s_ex")
        s_dt = sem("s_dt")
        s_rd = sem("s_rd")
        s_pn = sem("s_pn")
        s_tp = sem("s_tp")
        s_ph = sem("s_ph")
        s_pl = sem("s_pl")
        s_o = sem("s_o")
        s_oe = sem("s_oe")
        s_ge = [sem(f"s_ge{n}") for n in range(4)]
        s_ga = sem("s_ga")
        s_gr = sem("s_gr")
        s_gt = [sem(f"s_gt{n}") for n in range(4)]
        s_pve = sem("s_pve")
        s_add = sem("s_add")
        s_sum = sem("s_sum")
        s_d = sem("s_d")
        s_dh = sem("s_dh")
        s_dl = sem("s_dl")
        s_pwh = sem("s_pwh")
        s_pwl = sem("s_pwl")
        s_mix = sem("s_mix")
        s_me = sem("s_me")
        s_mh = sem("s_mh")
        s_ml = sem("s_ml")
        s_y = sem("s_y")
        s_ye = sem("s_ye")

        from_one = [s_me, s_wl, s_pwl, s_ye, s_d, s_blk, s_kbl, s_o, s_s, s_oe, s_dl, s_mix, s_tp,
                    s_qn, s_ex, s_pl, s_pve, *s_gt, s_free]

        block = ctx.enter_context(nc.Block())

        def product_done(eng, h, n):
            eng.wait_ge(s_blk, ONE + h * NBLK + n + TILE_BLKS)

        def x_tile(i):
            if i == 1:
                return META, 0, 4
            r = max(i - 1, 0)
            return P, META + P * r, 4 * r + (i > 1)

        def half_cols(n):
            return slice(n * SUB, (n + 1) * SUB)

        @block.sync
        def _(sp):
            sp.dma_start(cst[:, :], consts).then_inc(s_cst, 16)
            sp.dma_start(vec[:, :], vecs).then_inc(s_cst, 16)

            def load_block(h, n, slot, src):
                if not (isinstance(n, int) and n < RAW):
                    sp.wait_ge(s_wl, ONE + h * NBLK + (n - RAW + 1))
                else:
                    sp.wait_ge(s_wl, ONE + h * (NBLK - RAW + n + 1))
                sp.dma_start(raw[:, slot, :], src).then_inc(s_raw[slot], 16)

            with sp.Fori(0, HALVES) as h:
                sp.wait_ge(s_me, ONE + h * 2 * GROUPS)
                sp.dma_start(g_row, norm_g.partition_broadcast(P)).then_inc(s_g, 16)
                for i in range(XT):
                    if i >= 2:
                        sp.wait_ge(s_xt, h * XG + x_tile(i - 1)[2])
                    rows, first, _ = x_tile(i)
                    sp.dma_start(x_t[i % 2][0:rows, :],
                                 xcat[bass.ds(h * HALF + first, rows), :]).then_inc(s_x[i % 2], 16)
                    if i < 2:
                        for n in (2 * i, 2 * i + 1):
                            load_block(h, n, n, w_in[n, :, :])
                for n in range(RAW, KV_BLKS):
                    load_block(h, n, n % RAW, w_in[n, :, :])
                with sp.Fori(0, PAIRS) as j:
                    for b in range(TILE_BLKS):
                        n = KV_BLKS + j * TILE_BLKS + b
                        load_block(h, n, b % RAW, w_in[n, :, :])
                with sp.Fori(0, GROUPS) as g:
                    sp.wait_ge(s_kn, h + 1)
                    sp.wait_ge(s_pwl, ONE + h * GROUPS + g)
                    sp.dma_start(pw_raw.rearrange("p (a c) -> p a c", a=2),
                                 pool_w[g, :, :].rearrange("(a p) c -> p a c", p=P)).then_inc(s_pw, 16)
                    for b in range(G_BLKS):
                        n = KV_BLKS + Q_BLKS + g * G_BLKS + b
                        load_block(h, n, b % RAW, w_in[n, :, :])
                with sp.Fori(0, OB) as nb:
                    for k in range(KT):
                        load_block(h, IN_BLKS + nb * KT + k, k % RAW,
                                   w_out[k * P:(k + 1) * P, bass.ds(nb * BLK, BLK)])
                        if k == 8:
                            sp.wait_ge(s_ml, (h + 1) * KT)
                            for r in range(ROWT):
                                sp.wait_ge(s_ye, ONE + (h * OB + nb) * ROWT + 0)
                                sp.dma_start(mixed[:, r, :],
                                             xcat[bass.ds(h * HALF + META + P * r, P),
                                                  bass.ds(nb * BLK, BLK)]).then_inc(s_res[r], 16)

        @block.gpsimd
        def _(pool):
            for first in from_one:
                pool.sem_inc(first, ONE)
            pool.memset(kT[:, :], 0.0).then_inc(s_init, 1)
            pool.memset(vT[:, :], 0.0).then_inc(s_init, 1)
            pool.memset(qd_h[:, :, :, :].bitcast(f32), 0.0).then_inc(s_init, 1)
            pool.memset(qd_l[:, :, :, :].bitcast(f32), 0.0).then_inc(s_init, 1)
            ADDS = 2 * sum(range(GROUPS))
            with pool.Fori(0, HALVES) as h:
                chained = 0
                for g in range(GROUPS):
                    for jj in range(2):
                        pool.wait_ge(s_pve, ONE + (h * GROUPS + g) * 2 + jj + 1)
                        pool.wait_ge(s_d, ONE + (h * GROUPS + g) * 2 + jj)
                        src = pv[jj]
                        for lev in range(g + 1):
                            dst = psum_w[(g - lev) % 2]
                            step, lo = 2 ** lev, 2 ** (lev + 1) - 1
                            if lev:
                                pool.wait_ge(s_add, h * ADDS + chained)
                            ins = pool.tensor_tensor(dst[:, lo:COLS], src[:, lo:COLS],
                                                     src[:, lo - step:COLS - step], ALU.add)
                            if lev < g:
                                ins.then_inc(s_add, 1)
                                chained += 1
                            else:
                                ins.then_inc(s_sum, 1)
                            src = dst
                with pool.Fori(0, OB) as nb:
                    for r in range(ROWT):
                        pool.wait_ge(s_ye, ONE + (h * OB + nb) * ROWT + r + 1)
                        pool.dma_start(out[bass.ds(h * HALF + P * r, P), bass.ds(nb * BLK, BLK)],
                                       mixed[:, ROWT + r, :]).then_inc(s_out[r], 16)
                    for r in range(ROWT):
                        pool.wait_ge(s_out[r], 16 * (h * OB + nb + 1))
                        pool.sem_inc(s_free, 1)
            for r in range(ROWT):
                pool.wait_ge(s_out[r], 16 * HALVES * OB)

        @block.scalar
        def _(act):
            def copy(dst, src):
                return nc.scalar.activation(dst, src, ACT.Copy)

            def make_split(h, base4):
                def go(off):
                    slot = off % RAW
                    act.wait_ge(s_raw[slot], 16 * (h * (NBLK // RAW) + base4 + off // RAW + 1))
                    if isinstance(base4, int) and base4 * RAW + off < SPLIT:
                        act.wait_ge(s_blk, ONE + h * (NBLK - SPLIT + off + 1))
                    else:
                        act.wait_ge(s_blk, ONE + h * NBLK + base4 * RAW + (off - SPLIT + 1))
                    copy(wh[:, slot, :], raw[:, slot, :]).then_inc(s_wh, 1)
                return go

            act.wait_ge(s_cst, 32)
            act.wait_ge(s_init, 4)
            eps = cst[:, C_EPS:C_EPS + 1]
            with act.Fori(0, HALVES) as h:
                sp0 = make_split(h, 0)

                def stats(i):
                    rows = x_tile(i)[0]
                    act.wait_ge(s_x[i % 2], 16 * (h * (3 if i % 2 == 0 else 2) + i // 2 + 1))
                    nc.scalar.activation(junk[0:rows, :], x_t[i % 2][0:rows, :], ACT.Square,
                                         accum_out=xss[0:rows, i:i + 1]).then_inc(s_xsq, 1)
                    act.wait_ge(s_xsq, h * XT + i + 1)
                    nc.scalar.activation(xsd[0:rows, i:i + 1], xss[0:rows, i:i + 1], ACT.Sqrt,
                                         scale=1.0 / D, bias=eps[0:rows, :]).then_inc(s_xsd, 1)

                def x_high(i):
                    _, c0, n = x_tile(i)
                    if i == 0:
                        act.wait_ge(s_blk, ONE + h * NBLK)
                    if i == 1:
                        act.wait_ge(s_xt, h * XG + n + 1)
                        copy(act_h[:, :, 0:META],
                             PT[:, 0:KT * META].rearrange("p (k c) -> p k c", c=META)).then_inc(s_xh, 1)
                        return
                    for q in range(4):
                        act.wait_ge(s_xt, h * XG + n + q + 1)
                        copy(act_h[:, 4 * q:4 * q + 4, c0:c0 + P],
                             XB[q][:, :].rearrange("p (k c) -> p k c", c=P)).then_inc(s_xh, 1)

                stats(0)
                stats(1)
                for n in range(LEAD):
                    sp0(n)
                for i in range(XT):
                    x_high(i)
                    if i + 2 < XT:
                        stats(i + 2)

                act.wait_ge(s_kbl, ONE + h)
                copy(kT[:, 0:CHUNK], kT[:, HALF:HALF + CHUNK]).then_inc(s_kd, 1)
                copy(vT[:, 0:CHUNK], vT[:, HALF:HALF + CHUNK])
                for s in range(4):
                    sp0(s + LEAD)
                product_done(act, h, 0)
                for n in range(2):
                    nc.scalar.activation(k_sq[:, half_cols(n)], R[n][:, 0:SUB], ACT.Square).then_inc(s_ksq, 1)
                for s in range(4, KV_BLKS):
                    sp0(s + LEAD)
                act.wait_ge(s_kss, h + 1)
                for n, bank in enumerate((PT, PM)):
                    nc.scalar.activation(k_rs[:, half_cols(n)], bank[:, 0:SUB], ACT.Sqrt,
                                         scale=1.0 / HD, bias=eps).then_inc(s_ksd, 1)
                product_done(act, h, TILE_BLKS)
                copy(v_meta[:, bass.ds(h, 1), :], R[2][:, 0:META].unsqueeze(1)).then_inc(s_vT, 1)
                copy(vT[:, CHUNK:CHUNK + SUB - META], R[2][:, META:SUB]).then_inc(s_vT, 1)
                copy(vT[:, CHUNK + SUB - META:CHUNK + HALF], O[:, 0:SUB]).then_inc(s_vT, 1)
                act.wait_ge(s_vt, h + 1)
                copy(v_all, S[:, :, :].rearrange("p b (c n) -> p (b c) n", c=4)).then_inc(s_va, 1)
                copy(vm_all, R[2][0:META, 0:P]).then_inc(s_va, 1)
                act.wait_ge(s_kn, h + 1)
                for e in range(KVH):
                    for half in range(2):
                        src, dst = slice(e * HD, (e + 1) * HD), slice(half * HD, (half + 1) * HD)
                        copy(k_dup[dst, e, META:META + CHUNK + HALF], kT[src, :]).then_inc(s_kd, 1)
                        copy(k_dup[dst, e, 0:META], k_meta[src, 0, :]).then_inc(s_kd, 1)
                act.wait_ge(s_kd, (h + 1) * 9)
                kb = kb_h[:, :, :].rearrange("p e (c n) -> p e c n", n=BAND)
                for e in range(KVH):
                    copy(kb[:, e, :, 0:CHUNK],
                         k_dup[:, e, META:].rearrange("p (c n) -> p c n", n=CHUNK)).then_inc(s_kbh, 1)
                    copy(kb[:, e, :, CHUNK:BAND],
                         k_dup[:, e, 0:META].unsqueeze(1).to_broadcast([P, NCH + 1, META])).then_inc(s_kbh, 1)

                with act.Fori(0, PAIRS // 2) as jq:
                    spq = make_split(h, KV_BLKS // RAW + jq * 2)
                    for t in range(2):
                        for s in range(4):
                            spq(4 * t + s + LEAD)
                        product_done(act, h, KV_BLKS + (jq * 2 + t) * TILE_BLKS)
                        nc.scalar.activation(q_sq[t], R[t][:, :], ACT.Square).then_inc(s_qsq, 1)
                        act.wait_ge(s_qss, h * PAIRS + jq * 2 + t + 1)
                        nc.scalar.activation(q_rs[t], (PT, PM)[t][:, :], ACT.Sqrt,
                                             scale=1.0 / HD, bias=eps).then_inc(s_qsd, 1)

                with act.Fori(0, KVH) as e:
                    act.wait_ge(s_o, ONE + (h * KVH + e) * 2 * UNITS)
                    act.wait_ge(s_va, 2 * (h + 1))
                    for dup in range(2):
                        copy(v_h[:, :, dup, :], v_all[:, :, bass.ds(e * HD, HD)]).then_inc(s_vh, 1)
                        copy(vm_h[:, dup, :], vm_all[:, bass.ds(e * HD, HD)]).then_inc(s_vh, 1)
                    with act.Fori(0, 2) as gg:
                        g = e * 2 + gg
                        G = h * GROUPS + g
                        n0 = KV_BLKS + Q_BLKS + g * G_BLKS
                        spg = make_split(h, (KV_BLKS + Q_BLKS) // RAW + g * (G_BLKS // RAW))

                        def qdiag(u):
                            act.wait_ge(s_s, ONE + G * UNITS + u)
                            q = mixed[:, bass.ds(PAIRS + g * 2 + u // 2, 1),
                                      (u % 2) * 256:(u % 2) * 256 + 256].rearrange(
                                          "p a (c t) -> p (a c) t", t=CHUNK)
                            copy(qd_h[0:HD, :, 0, :], q[0:HD]).then_inc(s_qdh, 1)
                            copy(qd_h[HD:P, :, 1, :], q[HD:P]).then_inc(s_qdh, 1)

                        def exps(u):
                            act.wait_ge(s_nm, G * UNITS + u + 1)
                            sink = vec[:, bass.ds(V_SINK + g * 2 + u // 2, 1)]
                            for c in range(QUAD):
                                nc.scalar.activation(
                                    prob[:, c, :], S[:, c // 2, (c % 2) * KEYS:(c % 2 + 1) * KEYS], ACT.Exp,
                                    bias=nmax[:, c:c + 1], accum_out=den[:, c:c + 1]).then_inc(s_ex, 1)
                            nc.scalar.activation(esink[:, :], nmax[:, :], ACT.Exp, bias=sink).then_inc(s_ex, 1)

                        def p_high(u):
                            act.wait_ge(s_tp, ONE + G * UNITS + u + 1)
                            act.wait_ge(s_o, ONE + G * UNITS + u)
                            copy(pt_h[:, :], PT[:, :]).then_inc(s_ph, 1)
                            copy(pm_h[:, :], PM[0:META, :]).then_inc(s_ph, 1)

                        def gate_exp(n, bank):
                            product_done(act, h, n0 + (0, 4, 16, 20)[n])
                            if n < 2:
                                act.wait_ge(s_oe, ONE + G * UNITS)
                            else:
                                act.wait_ge(s_me, ONE + G * 2)
                            nc.scalar.activation(gate[n], bank[:, :], ACT.Exp, scale=-1.0).then_inc(s_ge[n], 1)

                        def pv_out(jj, banks):
                            product_done(act, h, n0 + 8 + 4 * jj)
                            act.wait_ge(s_dl, ONE + G * 2)
                            for n in range(2):
                                ins = copy(pv[jj][:, half_cols(n)], banks[n][:, 0:SUB])
                            ins.then_inc(s_pve, 1)

                        def d_high(jj):
                            act.wait_ge(s_d, ONE + G * 2 + jj + 1)
                            act.wait_ge(s_mix, ONE + G * 2)
                            copy(d_h[:, jj, :], pv[jj][:, META:COLS]).then_inc(s_dh, 1)

                        def pw_high():
                            act.wait_ge(s_pw, 16 * (G + 1))
                            act.wait_ge(s_mix, ONE + G * 2)
                            copy(pw_h[:, :], pw_raw).then_inc(s_pwh, 1)

                        todo = {s: [] for s in range(G_BLKS + 1)}
                        for u in range(UNITS):
                            todo[4 * u + 1].append((qdiag, u))
                            todo[4 * u + 5].append((exps, u))
                            todo[4 * u + 9].append((p_high, u))
                        todo[2].append((pw_high,))
                        todo[4].append((gate_exp, 0, R[0]))
                        todo[8].append((gate_exp, 1, R[1]))
                        todo[12].append((pv_out, 0, (R[2], R[0])))
                        todo[16].append((pv_out, 1, (R[1], R[2])))
                        todo[16].append((d_high, 0))
                        todo[20].append((gate_exp, 2, R[0]))
                        todo[20].append((d_high, 1))
                        todo[24].append((gate_exp, 3, R[1]))
                        for s in range(G_BLKS + 1):
                            if s < G_BLKS:
                                spg(s + LEAD)
                            for f, *a in todo[s]:
                                f(*a)

                act.wait_ge(s_blk, ONE + h * NBLK + IN_BLKS)
                act.wait_ge(s_oe, ONE + (h + 1) * GROUPS * UNITS)
                act.wait_ge(s_me, ONE + (h + 1) * GROUPS * 2)
                for k in range(KT):
                    copy(act_h[:, k, 0:HALF], mixed[:, k, :]).then_inc(s_mh, 1)
                with act.Fori(0, OB - 1) as nb:
                    spo = make_split(h, IN_BLKS // RAW + nb * (KT // RAW))
                    for s in range(KT):
                        spo(s + LEAD)
                spo = make_split(h, (IN_BLKS + (OB - 1) * KT) // RAW)
                for s in range(KT - LEAD):
                    spo(s + LEAD)

        @block.vector
        def _(dve):
            def sub(dst, a, b):
                return nc.vector.tensor_tensor(dst, a, b, ALU.subtract)

            def make_split(h, base4):
                def go(off):
                    slot = off % RAW
                    dve.wait_ge(s_wh, h * NBLK + base4 * RAW + off + 1)
                    sub(wl[:, slot, :], raw[:, slot, :], wh[:, slot, :]).then_inc(s_wl, 1)
                return go

            dve.wait_ge(s_cst, 32)
            dve.wait_ge(s_init, 4)
            nc.vector.tensor_scalar(gq8[:, :], vec[:, V_GQ:V_GQ + 1], HD ** -0.5, None, ALU.mult).then_inc(s_gq, 1)
            dve.wait_ge(s_gq, 1)
            with dve.Fori(0, HALVES) as h:
                sp0 = make_split(h, 0)

                def norm(i):
                    rows = x_tile(i)[0]
                    dve.wait_ge(s_xsd, h * XT + i + 1)
                    nc.vector.reciprocal(xrs[0:rows, i:i + 1], xsd[0:rows, i:i + 1]).then_inc(s_xrs, 1)
                    dve.wait_ge(s_xrs, h * XT + i + 1)
                    dve.wait_ge(s_g, 16 * (h + 1))
                    nc.vector.scalar_tensor_tensor(x_t[i % 2][0:rows, :], x_t[i % 2][0:rows, :],
                                                   xrs[0:rows, i:i + 1], g_row[0:rows, :],
                                                   ALU.mult, ALU.mult).then_inc(s_xn, 1)

                def x_low(i):
                    _, c0, n = x_tile(i)
                    if i == 1:
                        dve.wait_ge(s_xh, h * XG + n + 1)
                        sub(act_l[:, :, 0:META], PT[:, 0:KT * META].rearrange("p (k c) -> p k c", c=META),
                            act_h[:, :, 0:META]).then_inc(s_xl, 1)
                        return
                    for q in range(4):
                        dve.wait_ge(s_xh, h * XG + n + q + 1)
                        sub(act_l[:, 4 * q:4 * q + 4, c0:c0 + P],
                            XB[q][:, :].rearrange("p (k c) -> p k c", c=P),
                            act_h[:, 4 * q:4 * q + 4, c0:c0 + P]).then_inc(s_xl, 1)

                norm(0)
                norm(1)
                for n in range(LEAD):
                    sp0(n)
                for i in range(XT):
                    x_low(i)
                    if i + 2 < XT:
                        norm(i + 2)

                for s in range(KV_BLKS):
                    sp0(s + LEAD)
                dve.wait_ge(s_ksd, 2 * (h + 1))
                nc.vector.reciprocal(k_rs, k_rs).then_inc(s_krs, 1)
                dve.wait_ge(s_krs, h + 1)
                dve.wait_ge(s_kd, 9 * h + 1)
                gk = vec[:, V_GK:V_GK + 1]
                nc.vector.scalar_tensor_tensor(k_meta[:, bass.ds(h, 1), :], R[0][:, 0:META].unsqueeze(1), gk,
                                               k_rs[:, 0:META].unsqueeze(1), ALU.mult, ALU.mult)
                nc.vector.scalar_tensor_tensor(kT[:, CHUNK:CHUNK + SUB - META], R[0][:, META:SUB], gk,
                                               k_rs[:, META:SUB], ALU.mult, ALU.mult)
                nc.vector.scalar_tensor_tensor(kT[:, CHUNK + SUB - META:CHUNK + HALF], R[1][:, 0:SUB], gk,
                                               k_rs[:, SUB:COLS], ALU.mult, ALU.mult).then_inc(s_kn, 1)
                kb = kb_h[:, :, :].rearrange("p e (c n) -> p e c n", n=BAND)
                kl = kb_l[:, :, :].rearrange("p e (c n) -> p e c n", n=BAND)
                for e in range(KVH):
                    dve.wait_ge(s_kbh, 4 * h + 2 * e + 2)
                    sub(kl[:, e, :, 0:CHUNK], k_dup[:, e, META:].rearrange("p (c n) -> p c n", n=CHUNK),
                        kb[:, e, :, 0:CHUNK])
                    ins = sub(kl[:, e, :, CHUNK:BAND],
                              k_dup[:, e, 0:META].unsqueeze(1).to_broadcast([P, NCH + 1, META]),
                              kb[:, e, :, CHUNK:BAND])
                ins.then_inc(s_kbl, 1)

                with dve.Fori(0, PAIRS // 2) as jq:
                    spq = make_split(h, KV_BLKS // RAW + jq * 2)
                    for t in range(2):
                        n = h * PAIRS + jq * 2 + t
                        for s in range(4):
                            spq(4 * t + s + LEAD)
                        dve.wait_ge(s_qsd, n + 1)
                        nc.vector.reciprocal(q_rs[t], q_rs[t]).then_inc(s_qrs, 1)
                        dve.wait_ge(s_qrs, n + 1)
                        nc.vector.scalar_tensor_tensor(mixed[:, bass.ds(PAIRS + jq * 2 + t, 1), :],
                                                       R[t][:, :].unsqueeze(1), gq8[:, :],
                                                       q_rs[t].unsqueeze(1), ALU.mult, ALU.mult).then_inc(s_qn, 1)

                with dve.Fori(0, KVH) as e:
                    dve.wait_ge(s_vh, 4 * (h * KVH + e + 1))
                    for dup in range(2):
                        sub(v_l[:, :, dup, :], v_all[:, :, bass.ds(e * HD, HD)], v_h[:, :, dup, :])
                        ins = sub(vm_l[:, dup, :], vm_all[:, bass.ds(e * HD, HD)], vm_h[:, dup, :])
                    ins.then_inc(s_vl, 1)
                    with dve.Fori(0, 2) as gg:
                        g = e * 2 + gg
                        G = h * GROUPS + g
                        n0 = KV_BLKS + Q_BLKS + g * G_BLKS
                        spg = make_split(h, (KV_BLKS + Q_BLKS) // RAW + g * (G_BLKS // RAW))

                        def qdiag(u):
                            dve.wait_ge(s_qdh, (G * UNITS + u + 1) * 2)
                            q = mixed[:, bass.ds(PAIRS + g * 2 + u // 2, 1),
                                      (u % 2) * 256:(u % 2) * 256 + 256].rearrange(
                                          "p a (c t) -> p (a c) t", t=CHUNK)
                            sub(qd_l[0:HD, :, 0, :], q[0:HD], qd_h[0:HD, :, 0, :])
                            sub(qd_l[HD:P, :, 1, :], q[HD:P], qd_h[HD:P, :, 1, :]).then_inc(s_qdl, 1)

                        def row_max(u):
                            dve.wait_ge(s_s, ONE + G * UNITS + u + 1)
                            nc.vector.tensor_reduce(
                                smax[:, :].rearrange("p (b c) -> p b c", b=2),
                                S[:, :, 0:2 * KEYS].rearrange("p b (c k) -> p b c k", c=2),
                                AX.X, ALU.max).then_inc(s_mx, 1)
                            dve.wait_ge(s_mx, G * UNITS + u + 1)
                            sink = vec[:, bass.ds(V_SINK + g * 2 + u // 2, 1)]
                            nc.vector.tensor_scalar(nmax[:, :], smax[:, :], sink, -1.0,
                                                    ALU.max, ALU.mult).then_inc(s_nm, 1)

                        def normalise(u):
                            n = G * UNITS + u
                            dve.wait_ge(s_ex, ONE + (n + 1) * (QUAD + 1))
                            nc.vector.tensor_tensor(dtot[:, :], den[:, :], esink[:, :], ALU.add).then_inc(s_dt, 1)
                            dve.wait_ge(s_dt, n + 1)
                            nc.vector.reciprocal(rden[:, :], dtot[:, :]).then_inc(s_rd, 1)
                            dve.wait_ge(s_rd, n + 1)
                            dve.wait_ge(s_tp, ONE + n)
                            r = rden[:, :].unsqueeze(2)
                            pc = pn.rearrange("p (c k) -> p c k", c=QUAD)
                            nc.vector.tensor_tensor(pc[:, :, 0:CHUNK], prob[:, :, 0:CHUNK],
                                                    r.to_broadcast([P, QUAD, CHUNK]), ALU.mult)
                            nc.vector.tensor_tensor(pc[:, :, CHUNK:P], prob[:, :, BAND:KEYS],
                                                    r.to_broadcast([P, QUAD, CHUNK]), ALU.mult)
                            nc.vector.tensor_tensor(pnm.rearrange("p (c k) -> p c k", c=QUAD),
                                                    prob[:, :, CHUNK:BAND],
                                                    r.to_broadcast([P, QUAD, META]), ALU.mult).then_inc(s_pn, 1)

                        def p_low(u):
                            dve.wait_ge(s_ph, (G * UNITS + u + 1) * 2)
                            sub(pt_l[:, :], PT[:, :], pt_h[:, :])
                            sub(pm_l[:, :], PM[0:META, :], pm_h[:, :]).then_inc(s_pl, 1)

                        def o_out(u):
                            dve.wait_ge(s_o, ONE + G * UNITS + u + 1)
                            dve.wait_ge(s_gt[u // 2], ONE + G + 1)
                            cols = slice((u % 2) * 256, (u % 2) * 256 + 256)
                            o = O[:, :].rearrange("p (c e t) -> p c e t", e=2, t=CHUNK)
                            gt = gate[u // 2][:, cols].rearrange("p (c t) -> p c t", t=CHUNK)
                            dst = mixed[:, bass.ds(PAIRS + g * 2 + u // 2, 1), cols].rearrange(
                                "p a (c t) -> p (a c) t", t=CHUNK)
                            nc.vector.tensor_tensor(dst[0:HD], o[0:HD, :, 0, :], gt[0:HD], ALU.mult)
                            nc.vector.tensor_tensor(dst[HD:P], o[HD:P, :, 1, :], gt[HD:P],
                                                    ALU.mult).then_inc(s_oe, 1)

                        def silu(n, bank):
                            dve.wait_ge(s_ge[n], G + 1)
                            nc.vector.tensor_scalar(gate[n], gate[n], 1.0, None, ALU.add).then_inc(s_ga, 1)
                            dve.wait_ge(s_ga, G * 4 + n + 1)
                            nc.vector.reciprocal(gate[n], gate[n]).then_inc(s_gr, 1)
                            dve.wait_ge(s_gr, G * 4 + n + 1)
                            nc.vector.tensor_tensor(gate[n], bank[:, :], gate[n], ALU.mult).then_inc(s_gt[n], 1)

                        def pooled(jj):
                            dve.wait_ge(s_sum, G * 2 + jj + 1)
                            nc.vector.scalar_tensor_tensor(
                                pv[jj][:, META:COLS], psum_w[0][:, META:COLS],
                                cst[:, bass.ds(C_INVW + g, 1)], pv[jj][:, META:COLS],
                                ALU.mult, ALU.subtract).then_inc(s_d, 1)

                        def d_low(jj):
                            dve.wait_ge(s_dh, G * 2 + jj + 1)
                            sub(d_l[:, jj, :], pv[jj][:, META:COLS], d_h[:, jj, :]).then_inc(s_dl, 1)

                        def pw_low():
                            dve.wait_ge(s_pwh, G + 1)
                            sub(pw_l[:, :], pw_raw, pw_h[:, :]).then_inc(s_pwl, 1)

                        def mix_out(jj, bank):
                            dve.wait_ge(s_mix, ONE + G * 2 + jj + 1)
                            dve.wait_ge(s_gt[2 + jj], ONE + G + 1)
                            dve.wait_ge(s_free, ONE + h * (OB * ROWT))
                            nc.vector.scalar_tensor_tensor(
                                mixed[:, bass.ds(g * 2 + jj, 1), :], bank[:, :].unsqueeze(1),
                                vec[:, bass.ds(V_SCALE + g * 2 + jj, 1)], gate[2 + jj].unsqueeze(1),
                                ALU.mult, ALU.mult).then_inc(s_me, 1)

                        todo = {s: [] for s in range(G_BLKS + 1)}
                        for u in range(UNITS):
                            todo[4 * u + 1].append((qdiag, u))
                            todo[4 * u + 4].append((row_max, u))
                            todo[4 * u + 6].append((normalise, u))
                            todo[4 * u + 9].append((p_low, u))
                            todo[4 * u + 11].append((o_out, u))
                        todo[2].append((pw_low,))
                        todo[5].append((silu, 0, R[0]))
                        todo[9].append((silu, 1, R[1]))
                        todo[15].append((pooled, 0))
                        todo[17].append((d_low, 0))
                        todo[19].append((pooled, 1))
                        todo[21].append((d_low, 1))
                        todo[21].append((silu, 2, R[0]))
                        todo[24].append((silu, 3, R[1]))
                        todo[24].append((mix_out, 0, PT))
                        todo[24].append((mix_out, 1, O))
                        for s in range(G_BLKS + 1):
                            if s < G_BLKS:
                                spg(s + LEAD)
                            for f, *a in todo[s]:
                                f(*a)

                for k in range(KT):
                    dve.wait_ge(s_mh, h * KT + k + 1)
                    sub(act_l[:, k, 0:HALF], mixed[:, k, :], act_h[:, k, 0:HALF]).then_inc(s_ml, 1)

                def y_out(nb):
                    for r in range(ROWT):
                        if r < ROWT - 1:
                            dve.wait_ge(s_y, (h * OB + nb) * (ROWT - 1) + r + 1)
                        else:
                            dve.wait_ge(s_blk, ONE + h * NBLK + IN_BLKS + (nb + 1) * KT)
                        dve.wait_ge(s_res[r], 16 * (h * OB + nb + 1))
                        dve.wait_ge(s_free, ONE + (h * OB + nb) * ROWT)
                        nc.vector.tensor_tensor(mixed[:, ROWT + r, :], XB[r][:, :], mixed[:, r, :],
                                                ALU.add).then_inc(s_ye, 1)

                with dve.Fori(0, OB - 1) as nb:
                    spo = make_split(h, IN_BLKS // RAW + nb * (KT // RAW))
                    for s in range(KT):
                        spo(s + LEAD)
                    y_out(nb)
                spo = make_split(h, (IN_BLKS + (OB - 1) * KT) // RAW)
                for s in range(KT - LEAD):
                    spo(s + LEAD)
                y_out(OB - 1)

        @block.tensor
        def _(pe):
            mm = nc.tensor.matmul

            def tile(h, n, banks, cols, start_blk=0, events=None, slot0=0):
                for b in range(TILE_BLKS):
                    pe.wait_ge(s_wl, ONE + h * NBLK + n + b + 1)
                    for kk in range(4):
                        k = 4 * b + kk
                        w = slice(kk * P, (kk + 1) * P)
                        for bank, c in zip(banks, cols):
                            o = bank[:, 0:c.stop - c.start]
                            mm(o, wh[:, b, w], act_h[:, k, c], start=(k == 0), stop=False)
                            mm(o, wh[:, b, w], act_l[:, k, c], start=False, stop=False)
                        for bank, c in zip(banks, cols):
                            o = bank[:, 0:c.stop - c.start]
                            last = mm(o, wl[:, b, w], act_h[:, k, c], start=False, stop=(k == KT - 1))
                    last.then_inc(s_blk, 1)
                    if events:
                        events(slot0 + b)
                return last

            both = (half_cols(0), half_cols(1))
            own = (slice(META, COLS),)

            pe.wait_ge(s_cst, 32)
            pe.wait_ge(s_init, 4)
            with pe.Fori(0, HALVES) as h:
                pe.wait_ge(s_ye, ONE + h * OB * ROWT)
                for i in range(XT):
                    if i != 1:
                        pe.wait_ge(s_xn, h * XT + i + 1)
                    if i == 1:
                        for k in range(KT):
                            last = nc.tensor.transpose(PT[:, k * META:(k + 1) * META],
                                                       x_t[1][0:META, k * P:(k + 1) * P],
                                                       ident[0:META, 0:META])
                        last.then_inc(s_xt, 1)
                        continue
                    for q in range(4):
                        if i > 1:
                            pe.wait_ge(s_xl, h * XG + x_tile(0 if i == 2 else i - 1)[2] + q + 1)
                        if i == 0 and q == 3:
                            pe.wait_ge(s_xn, h * XT + 2)
                        for kk in range(4):
                            k = 4 * q + kk
                            last = nc.tensor.transpose(XB[q][:, kk * P:(kk + 1) * P],
                                                       x_t[i % 2][:, k * P:(k + 1) * P], ident)
                        last.then_inc(s_xt, 1)

                pe.wait_ge(s_xl, (h + 1) * XG)
                tile(h, 0, (R[0], R[1]), both)
                tile(h, TILE_BLKS, (R[2], O), both)
                pe.wait_ge(s_ksq, 2 * (h + 1))
                for n, bank in enumerate((PT, PM)):
                    last = mm(bank[:, 0:SUB], blkones, k_sq[:, half_cols(n)], start=True, stop=True)
                last.then_inc(s_kss, 1)
                pe.wait_ge(s_vT, 3 * (h + 1))
                for c in range(NCH):
                    nc.tensor.transpose(S[:, c // 4, (c % 4) * P:(c % 4 + 1) * P],
                                        vT[:, c * CHUNK:c * CHUNK + P], ident)
                nc.tensor.transpose(R[2][0:META, 0:P], v_meta[:, 0, :], ident).then_inc(s_vt, 1)

                with pe.Fori(0, PAIRS // 2) as jq:
                    pe.wait_ge(s_kn, h + 1)
                    pe.wait_ge(s_qn, ONE + h * PAIRS + jq * 2)
                    for t in range(2):
                        tile(h, KV_BLKS + (jq * 2 + t) * TILE_BLKS, (R[t],), own)
                        pe.wait_ge(s_qsq, h * PAIRS + jq * 2 + t + 1)
                        mm((PT, PM)[t][:, :], blkones, q_sq[t], start=True, stop=True).then_inc(s_qss, 1)

                with pe.Fori(0, KVH) as e:
                    with pe.Fori(0, 2) as gg:
                        g = e * 2 + gg
                        G = h * GROUPS + g

                        def scores(u):
                            pe.wait_ge(s_qdl, G * UNITS + u + 1)
                            pe.wait_ge(s_ex, ONE + (G * UNITS + u) * (QUAD + 1))
                            pe.wait_ge(s_kbl, ONE + h + 1)
                            for c in range(QUAD):
                                ch = (u % 2) * QUAD + c
                                o = S[:, c // 2, (c % 2) * KEYS:(c % 2 + 1) * KEYS]
                                keys_h = kb_h[:, bass.ds(e, 1), ch * BAND:ch * BAND + KEYS].rearrange("p a k -> p (a k)")
                                keys_l = kb_l[:, bass.ds(e, 1), ch * BAND:ch * BAND + KEYS].rearrange("p a k -> p (a k)")
                                qh = qd_h[:, c, :, :].rearrange("p a t -> p (a t)")
                                ql = qd_l[:, c, :, :].rearrange("p a t -> p (a t)")
                                mm(o, qh, keys_h, start=True, stop=False)
                                mm(o, qh, keys_l, start=False, stop=False)
                                last = mm(o, ql, keys_h, start=False, stop=(ch > 0))
                                if ch == 0:
                                    last = mm(o, ones_row, cst[0:1, bass.ds(C_MASK + h * KEYS, KEYS)],
                                              start=False, stop=True)
                            last.then_inc(s_s, 1)

                        def transposes(u):
                            n = G * UNITS + u
                            pe.wait_ge(s_pn, n + 1)
                            pe.wait_ge(s_pl, ONE + n)
                            pe.wait_ge(s_me, ONE + G * 2)
                            for c in range(QUAD):
                                nc.tensor.transpose(PT[:, c * P:(c + 1) * P], pn[:, c * P:(c + 1) * P], ident)
                            for c in range(QUAD):
                                last = nc.tensor.transpose(PM[0:META, c * P:(c + 1) * P],
                                                           pnm[:, c * META:(c + 1) * META], ident)
                            last.then_inc(s_tp, 1)

                        def values(u):
                            n = G * UNITS + u
                            pe.wait_ge(s_pl, ONE + n + 1)
                            pe.wait_ge(s_vl, h * KVH + e + 1)
                            pe.wait_ge(s_oe, ONE + n)
                            vmh = vm_h[:, :, :].rearrange("p a d -> p (a d)")
                            vml = vm_l[:, :, :].rearrange("p a d -> p (a d)")
                            mm(O[:, :], vmh, pm_h[:, :], start=True, stop=False)
                            mm(O[:, :], vmh, pm_l[:, :], start=False, stop=False)
                            mm(O[:, :], vml, pm_h[:, :], start=False, stop=False)
                            for c in range(QUAD):
                                ch = (u % 2) * QUAD + c
                                cs = slice(c * P, (c + 1) * P)
                                vh = v_h[:, ch, :, :].rearrange("p a d -> p (a d)")
                                vl = v_l[:, ch, :, :].rearrange("p a d -> p (a d)")
                                mm(O[:, cs], vh, pt_h[:, cs], start=False, stop=False)
                                mm(O[:, cs], vh, pt_l[:, cs], start=False, stop=False)
                                last = mm(O[:, cs], vl, pt_h[:, cs], start=False, stop=(c == QUAD - 1))
                            last.then_inc(s_o, 1)

                        when = {}
                        for u in range(UNITS):
                            when.setdefault(4 * u + 3, []).append((scores, u))
                            when.setdefault(4 * u + 8, []).append((transposes, u))
                            when.setdefault(4 * u + 10, []).append((values, u))

                        def events(s):
                            for f, u in when.get(s, ()):
                                f(u)

                        n0 = KV_BLKS + Q_BLKS + g * G_BLKS
                        pe.wait_ge(s_qn, ONE + (h + 1) * PAIRS)
                        pe.wait_ge(s_va, 2 * (h + 1))
                        pe.wait_ge(s_gt[2], ONE + G)
                        tile(h, n0, (R[0],), own, events=events, slot0=0)
                        pe.wait_ge(s_gt[3], ONE + G)
                        tile(h, n0 + 4, (R[1],), own, events=events, slot0=4)
                        pe.wait_ge(s_gt[0], ONE + G + 1)
                        pe.wait_ge(s_pve, ONE + G * 2)
                        tile(h, n0 + 8, (R[2], R[0]), both, events=events, slot0=8)
                        pe.wait_ge(s_gt[1], ONE + G + 1)
                        pe.wait_ge(s_pve, ONE + G * 2 + 1)
                        tile(h, n0 + 12, (R[1], R[2]), both, events=events, slot0=12)
                        tile(h, n0 + 16, (R[0],), own, events=events, slot0=16)
                        pe.wait_ge(s_pve, ONE + G * 2 + 2)
                        tile(h, n0 + 20, (R[1],), own, events=events, slot0=20)
                        pe.wait_ge(s_dl, ONE + G * 2 + 2)
                        pe.wait_ge(s_pwl, ONE + G + 1)
                        for jj, bank in enumerate((PT, O)):
                            if jj == 0:
                                pe.wait_ge(s_pl, ONE + (G + 1) * UNITS)
                            else:
                                pe.wait_ge(s_oe, ONE + (G + 1) * UNITS)
                            for a in range(2):
                                w = slice(a * 256 + jj * P, a * 256 + (jj + 1) * P)
                                mm(bank[:, :], pw_h[:, w], d_h[:, a, :], start=(a == 0), stop=False)
                                mm(bank[:, :], pw_h[:, w], d_l[:, a, :], start=False, stop=False)
                                last = mm(bank[:, :], pw_l[:, w], d_h[:, a, :], start=False, stop=(a == 1))
                            last.then_inc(s_mix, 1)

                with pe.Fori(0, OB) as nb:
                    for k in range(KT):
                        n = IN_BLKS + nb * KT + k
                        pe.wait_ge(s_ml, h * KT + k + 1)
                        pe.wait_ge(s_wl, ONE + h * NBLK + n + 1)
                        for r in range(ROWT):
                            if k == 0:
                                pe.wait_ge(s_ye, ONE + (h * OB + nb) * ROWT)
                            c = slice(r * P, (r + 1) * P)
                            mm(XB[r][:, :], act_h[:, k, c], wh[:, k % SPLIT, :], start=(k == 0), stop=False)
                            mm(XB[r][:, :], act_h[:, k, c], wl[:, k % SPLIT, :], start=False, stop=False)
                            last = mm(XB[r][:, :], act_l[:, k, c], wh[:, k % SPLIT, :], start=False,
                                      stop=(k == KT - 1))
                            if k == KT - 1 and r < ROWT - 1:
                                last.then_inc(s_y, 1)
                        last.then_inc(s_blk, 1)



def _block_layout(w_in):
    import numpy as np
    tiles = [24, 25] + list(range(16, 24))
    for g in range(GROUPS):
        tiles += [26 + 2 * g, 27 + 2 * g, 2 * g, 2 * g + 1, 8 + 2 * g, 9 + 2 * g]
    w = w_in.reshape(4, 4, P, -1, P)
    w = w[:, :, :, tiles, :].transpose(3, 0, 2, 1, 4)
    return np.ascontiguousarray(w).reshape(len(tiles) * 4, P, BLK)


def _constants():
    import numpy as np
    c = np.zeros((P, C_N), np.float32)
    c[:, C_ID:C_ID + P] = np.eye(P)
    c[:, C_BLK:C_BLK + P] = np.kron(np.eye(2), np.ones((HD, HD)))
    c[:, C_ONE:C_ONE + P] = 1.0
    c[:, C_MASK:C_MASK + CHUNK] = MASKED
    for g in range(GROUPS):
        c[:, C_INVW + g] = 0.5 ** (g + 1)
    c[:, C_EPS] = EPS
    return c


def kernel(x, meta_tokens, norm_g, w_in, pool_w, pool_scale, q_norm_g, k_norm_g, sinks, w_out):
    import numpy as np
    import concourse.bacc as bacc
    from concourse.bass_utils import run_bass_kernel_spmd

    a = lambda t: np.asarray(t)
    vecs = np.concatenate([
        a(pool_scale)[0].reshape(PAIRS, P).T,
        np.repeat(a(sinks)[0].reshape(PAIRS, 2).T, HD, axis=0),
        np.tile(a(q_norm_g)[0], 2)[:, None],
        np.tile(a(k_norm_g)[0], 2)[:, None]], axis=1)
    arrays = {
        "xcat": np.concatenate([a(meta_tokens), a(x)[0]], axis=0),
        "norm_g_in": a(norm_g)[0],
        "w_in_blocks": _block_layout(a(w_in)[0]),
        "w_out_in": a(w_out)[0],
        "pool_w_in": a(pool_w)[0],
        "vecs": vecs,
        "consts": _constants(),
    }
    arrays = {n: np.ascontiguousarray(v) for n, v in arrays.items()}
    nc = bacc.Bacc("TRN2", target_bir_lowering=False, num_devices=1)
    args = [nc.dram_tensor(n, v.shape, mybir.dt.from_np(v.dtype), kind="ExternalInput").ap()
            for n, v in arrays.items()]
    out = nc.dram_tensor("out", (SEQ, D), mybir.dt.float32, kind="ExternalOutput").ap()
    hymba_layer(nc, *args, out)
    got = run_bass_kernel_spmd(nc, [arrays], core_ids=[0]).results[0]["out"]
    return np.asarray(got).reshape(1, SEQ, D)
```

```python
from contextlib import ExitStack

import concourse.bass as bass
from concourse import mybir

P = 128
D = 2048
KT = D // P
META = 16
SEQ = 1024
HALF = 512
HALVES = SEQ // HALF
COLS = META + HALF
SUB = COLS // 2
CHUNK = 64
NCH = HALF // CHUNK
HD = 64
PAIRS = 8
KVH = 2
GROUPS = 4
QUAD = 4
BAND = META + CHUNK
KEYS = BAND + CHUNK
EPS = 1e-6
MASKED = -1e30
ONE = 1
QB_FREE = 4

BLK = 512
TILE_BLKS = 4
RAW = 4
SPLIT = 4
LEAD = 3
KV_BLKS = 2 * TILE_BLKS
Q_BLKS = PAIRS * TILE_BLKS
G_BLKS = 6 * TILE_BLKS
IN_BLKS = KV_BLKS + Q_BLKS + GROUPS * G_BLKS
OB = D // BLK
OUT_BLKS = OB * KT
NBLK = IN_BLKS + OUT_BLKS
ROWT = HALF // P
XG = 4
K_ORDER = [0, 1, 2, 3, 4, 5, 8, 9, 10, 11, 12, 13, 6, 7, 14, 15]
UNITS = 4

C_ID, C_BLK, C_ONE, C_MASK = 0, 128, 256, 384
C_INVW = C_MASK + KEYS
C_EPS = C_INVW + GROUPS
C_N = C_EPS + 1
V_SCALE, V_SINK, V_GQ, V_GK = 0, 8, 16, 17
V_N = 18


def hymba_layer(nc, xcat, norm_g, w_in, w_out, pool_w, vecs, consts, out):
    f32, f32r, bf16 = mybir.dt.float32, mybir.dt.float32r, mybir.dt.bfloat16
    ACT = mybir.ActivationFunctionType
    ALU = mybir.AluOpType
    AX = mybir.AxisListType

    ctx = ExitStack()
    with ctx:
        def sb(name, shape, dt=f32):
            return ctx.enter_context(nc.sbuf_tensor(name, shape, dt))

        def sem(name):
            return ctx.enter_context(nc.semaphore(name))

        act_h = sb("act_h", [P, KT, COLS], f32r)
        act_l = sb("act_l", [P, KT, COLS], f32r)
        mixed = sb("mixed", [P, KT, HALF])
        raw = sb("raw", [P, RAW, BLK])
        wh = sb("wh", [P, SPLIT, BLK], f32r)
        wl = sb("wl", [P, SPLIT, BLK], f32r)
        kT = sb("kT", [P, CHUNK + HALF])
        vT = sb("vT", [P, CHUNK + HALF])
        k_meta = sb("k_meta", [P, HALVES, META])
        v_meta = sb("v_meta", [P, HALVES, META])
        cst = sb("cst", [P, C_N])
        vec = sb("vec", [P, V_N])
        gq8 = sb("gq8", [P, 1])
        junk = sb("junk", [P, D], bf16)
        xss = sb("xss", [P, 2])
        xsd = sb("xsd", [P, 2])
        xrs = sb("xrs", [P, 2])
        kb_h = sb("kb_h", [P, KVH, (NCH + 1) * BAND], f32r)
        kb_l = sb("kb_l", [P, KVH, (NCH + 1) * BAND], f32r)
        v_h = sb("v_h", [P, NCH, 2, HD], f32r)
        v_l = sb("v_l", [P, NCH, 2, HD], f32r)
        vm = sb("vm", [96, 2, HD], f32r)
        pm = sb("pm", [96, QUAD * P], f32r)
        qd_h = sb("qd_h", [P, QUAD, 2, CHUNK], f32r)
        qd_l = sb("qd_l", [P, QUAD, 2, CHUNK], f32r)
        pt_h = sb("pt_h", [P, QUAD * P], f32r)
        pt_l = sb("pt_l", [P, QUAD * P], f32r)
        d_h = sb("d_h", [P, 2, HALF], f32r)
        d_l = sb("d_l", [P, 2, HALF], f32r)
        pw_h = sb("pw_h", [P, BLK], f32r)
        pw_l = sb("pw_l", [P, BLK], f32r)
        smax = sb("smax", [P, QUAD])
        nmax = sb("nmax", [P, QUAD])
        den = sb("den", [P, QUAD])
        esink = sb("esink", [P, QUAD])
        dtot = sb("dtot", [P, QUAD])
        rden = sb("rden", [P, QUAD])

        scr = sb("scr", [P, 7168])
        x_t = [scr[:, 0:D], scr[:, D:2 * D]]
        g_row = scr[:, 2 * D:3 * D]
        res2 = sb("res2", [P, 2, BLK])
        y = [scr[:, 3 * D:3 * D + BLK], scr[:, 3 * D + BLK:3 * D + 2 * BLK], res2[:, 0, :], res2[:, 1, :]]
        mix_h = [kb_h[:, 0, 0:BLK], kb_h[:, 1, 0:BLK],
                 v_h[:, 0:4, :, :].rearrange("p c a d -> p (c a d)"),
                 v_h[:, 4:8, :, :].rearrange("p c a d -> p (c a d)")]
        mix_l = [kb_l[:, 0, 0:BLK], kb_l[:, 1, 0:BLK],
                 v_l[:, 0:4, :, :].rearrange("p c a d -> p (c a d)"),
                 v_l[:, 4:8, :, :].rearrange("p c a d -> p (c a d)")]
        k_dup = scr[:, 0:1184].rearrange("p (h c) -> p h c", h=KVH)
        k_sq, k_rs = scr[:, 1184:1712], scr[:, 1712:2240]
        q_sq = [scr[:, 2240:2752], scr[:, 2752:3264]]
        q_rs = [scr[:, 3264:3776], scr[:, 3776:4288]]
        prob = scr[:, 0:QUAD * KEYS].rearrange("p (c k) -> p c k", c=QUAD)
        pn = scr[:, 576:1088]
        pnm = scr[:, 1088:1152]
        gate = [scr[:, 1152 + HALF * n:1152 + HALF * (n + 1)] for n in range(4)]
        pv = [scr[:, 3200:3728], scr[:, 3728:4256]]
        v_all = scr[:, 4288:5312].rearrange("p (c n) -> p c n", c=NCH)
        psum_w = [scr[:, 5312:5840], scr[:, 5840:6368]]
        pw_raw = scr[:, 6368:6880]
        vm_all = scr[0:META, 6880:7008]

        R = [ctx.enter_context(nc.psum_tensor(f"R{i}", [P, BLK], f32)) for i in range(3)]
        S = ctx.enter_context(nc.psum_tensor("S", [P, 2, BLK], f32))
        PT = ctx.enter_context(nc.psum_tensor("PT", [P, BLK], f32))
        PM = ctx.enter_context(nc.psum_tensor("PM", [P, BLK], f32))
        O = ctx.enter_context(nc.psum_tensor("O", [P, BLK], f32))
        YB = [R[0], R[1], R[2], O]
        XB = [S[:, 0, :], S[:, 1, :], PT[:, :], PM[:, :]]
        QB = [O, R[2], R[0], R[1]]

        ident = cst[:, C_ID:C_ID + P]
        blkones = cst[:, C_BLK:C_BLK + P]
        ones_row = cst[0:1, C_ONE:C_ONE + P]

        s_cst = sem("s_cst")
        s_g = sem("s_g")
        s_g2 = sem("s_g2")
        s_x = [sem(f"s_x{i}") for i in range(2)]
        s_raw = [sem(f"s_raw{i}") for i in range(RAW)]
        s_pw = sem("s_pw")
        s_res = [sem(f"s_res{i}") for i in range(ROWT)]
        s_out = [sem(f"s_out{i}") for i in range(ROWT)]
        s_free = sem("s_free")
        s_init = sem("s_init")
        s_gq = sem("s_gq")
        s_wh = sem("s_wh")
        s_wl = sem("s_wl")
        s_blk = sem("s_blk")
        s_xsq = sem("s_xsq")
        s_xsd = sem("s_xsd")
        s_xrs = sem("s_xrs")
        s_xn = sem("s_xn")
        s_xt = sem("s_xt")
        s_xh = sem("s_xh")
        s_xl = sem("s_xl")
        s_ksq = sem("s_ksq")
        s_kss = sem("s_kss")
        s_ksd = sem("s_ksd")
        s_krs = sem("s_krs")
        s_kn = sem("s_kn")
        s_kd = sem("s_kd")
        s_kbh = sem("s_kbh")
        s_kbl = sem("s_kbl")
        s_vT = sem("s_vT")
        s_vt = sem("s_vt")
        s_va = sem("s_va")
        s_vh = sem("s_vh")
        s_vl = sem("s_vl")
        s_qsq = sem("s_qsq")
        s_qss = sem("s_qss")
        s_qsd = sem("s_qsd")
        s_qrs = sem("s_qrs")
        s_qn = sem("s_qn")
        s_qdh = sem("s_qdh")
        s_qdl = sem("s_qdl")
        s_s = sem("s_s")
        s_mx = sem("s_mx")
        s_nm = sem("s_nm")
        s_ex = sem("s_ex")
        s_dt = sem("s_dt")
        s_rd = sem("s_rd")
        s_pn = sem("s_pn")
        s_tp = sem("s_tp")
        s_ph = sem("s_ph")
        s_pl = sem("s_pl")
        s_o = sem("s_o")
        s_oe = sem("s_oe")
        s_ge = [sem(f"s_ge{n}") for n in range(4)]
        s_ga = sem("s_ga")
        s_gr = sem("s_gr")
        s_gt = [sem(f"s_gt{n}") for n in range(4)]
        s_pve = sem("s_pve")
        s_add = sem("s_add")
        s_sum = sem("s_sum")
        s_d = sem("s_d")
        s_dh = sem("s_dh")
        s_dl = sem("s_dl")
        s_pwh = sem("s_pwh")
        s_pwl = sem("s_pwl")
        s_mix = sem("s_mix")
        s_me = sem("s_me")
        s_mh = sem("s_mh")
        s_ml = sem("s_ml")
        s_y = sem("s_y")
        s_ye = sem("s_ye")

        from_one = [s_me, s_wl, s_pwl, s_ye, s_d, s_blk, s_kbl, s_o, s_s, s_oe, s_dl, s_mix, s_tp,
                    s_ex, s_pl, s_pve, *s_gt, s_free]

        block = ctx.enter_context(nc.Block())

        def product_done(eng, h, n):
            eng.wait_ge(s_blk, ONE + h * NBLK + n + TILE_BLKS)

        def half_cols(n):
            return slice(n * SUB, (n + 1) * SUB)

        @block.sync
        def _(sp):
            def load_block(n, slot, src, free=True):
                if free:
                    sp.wait_ge(s_wl, ONE + n - RAW + 1)
                sp.dma_start(raw[:, slot, :], src).then_inc(s_raw[slot], 16)

            def load_x(slot, row):
                sp.dma_start(x_t[slot], xcat[bass.ds(row, P), :]).then_inc(s_x[slot], 16)

            sp.dma_start(x_t[1][0:META, :], xcat[0:META, :]).then_inc(s_x[1], 16)
            load_x(0, META)
            sp.dma_start(cst[:, :], consts).then_inc(s_cst, 16)
            sp.dma_start(vec[:, :], vecs).then_inc(s_cst, 16)
            sp.dma_start(g_row, norm_g.partition_broadcast(P)).then_inc(s_g, 16)
            for n in range(RAW):
                load_block(n, n, w_in[n, :, :], free=False)
            for r in range(1, ROWT):
                sp.wait_ge(s_xt, 1 + XG * (r - 1))
                load_x(r % 2, META + P * r)

            for h in range(HALVES):
                h0 = h * NBLK
                for n in range(RAW if h == 0 else 0, KV_BLKS):
                    load_block(h0 + n, n % RAW, w_in[n, :, :])
                with sp.Fori(0, PAIRS) as j:
                    for b in range(TILE_BLKS):
                        n = KV_BLKS + j * TILE_BLKS + b
                        load_block(h0 + n, b % RAW, w_in[n, :, :])
                sp.wait_ge(s_free, ONE + h * OB * ROWT)
                with sp.Fori(0, GROUPS) as g:
                    sp.wait_ge(s_pwl, ONE + h * GROUPS + g)
                    sp.dma_start(pw_raw.rearrange("p (a c) -> p a c", a=2),
                                 pool_w[g, :, :].rearrange("(a p) c -> p a c", p=P)).then_inc(s_pw, 16)
                    for b in range(G_BLKS):
                        n = KV_BLKS + Q_BLKS + g * G_BLKS + b
                        load_block(h0 + n, b % RAW, w_in[n, :, :])

                def out_loads(nb, frames):
                    for k in range(KT):
                        kk = K_ORDER[k]
                        load_block(h0 + IN_BLKS + nb * KT + k, k % RAW,
                                   w_out[kk * P:(kk + 1) * P, bass.ds(nb * BLK, BLK)])
                        if k == RAW - 1 and frames is not None:
                            sp.wait_ge(s_me, ONE + (h + 1) * 2 * GROUPS)
                            sp.wait_ge(s_xt, 1 + XG * (ROWT - 1 + nb))
                            load_x(frames, HALF + META + P * nb)
                        if k == 8:
                            sp.wait_ge(s_me, ONE + (h + 1) * 2 * GROUPS)
                            sp.wait_ge(s_free, ONE + (h * OB + nb) * ROWT)
                            for r in range(ROWT):
                                sp.dma_start(y[r], xcat[h * HALF + META + P * r:h * HALF + META + P * (r + 1),
                                                        bass.ds(nb * BLK, BLK)]).then_inc(s_res[r], 16)

                if h == 0:
                    with sp.Fori(0, 2) as i:
                        for v in range(2):
                            nb = i * 2 + v
                            out_loads(nb, v)
                else:
                    with sp.Fori(0, OB) as nb:
                        out_loads(nb, None)

        @block.gpsimd
        def _(pool):
            for first in from_one:
                pool.sem_inc(first, ONE)
            pool.sem_inc(s_qn, QB_FREE)
            pool.memset(kT[:, :], 0.0).then_inc(s_init, 1)
            pool.memset(vT[:, :], 0.0).then_inc(s_init, 1)
            pool.memset(qd_h[:, :, :, :].bitcast(f32), 0.0).then_inc(s_init, 1)
            pool.memset(qd_l[:, :, :, :].bitcast(f32), 0.0).then_inc(s_init, 1)
            pool.memset(vm[:, :, :].bitcast(f32), 0.0).then_inc(s_init, 1)
            pool.memset(pm[:, :].bitcast(f32), 0.0).then_inc(s_init, 1)
            chained = 0
            for h in range(HALVES):
                for g in range(GROUPS):
                    for jj in range(2):
                        pool.wait_ge(s_pve, ONE + (h * GROUPS + g) * 2 + jj + 1)
                        pool.wait_ge(s_d, ONE + (h * GROUPS + g) * 2 + jj)
                        src = pv[jj]
                        for lev in range(g + 1):
                            dst = psum_w[(g - lev) % 2]
                            step, lo = 2 ** lev, 2 ** (lev + 1) - 1
                            if lev:
                                pool.wait_ge(s_add, chained)
                            ins = pool.tensor_tensor(dst[:, lo:COLS], src[:, lo:COLS],
                                                     src[:, lo - step:COLS - step], ALU.add)
                            if lev < g:
                                ins.then_inc(s_add, 1)
                                chained += 1
                            else:
                                ins.then_inc(s_sum, 1)
                            src = dst
                if h == 0:
                    pool.wait_ge(s_me, ONE + 2 * GROUPS)
                    pool.dma_start(g_row, norm_g.partition_broadcast(P)).then_inc(s_g2, 16)
                with pool.Fori(0, OB) as nb:
                    for r in range(ROWT):
                        pool.wait_ge(s_ye, ONE + (h * OB + nb) * ROWT + r + 1)
                        pool.dma_start(out[h * HALF + P * r:h * HALF + P * (r + 1), bass.ds(nb * BLK, BLK)],
                                       y[r]).then_inc(s_out[r], 16)
                    for r in range(ROWT):
                        pool.wait_ge(s_out[r], 16 * (h * OB + nb + 1))
                        pool.sem_inc(s_free, 1)
            for r in range(ROWT):
                pool.wait_ge(s_out[r], 16 * HALVES * OB)

        @block.scalar
        def _(act):
            def copy(dst, src):
                return nc.scalar.activation(dst, src, ACT.Copy)

            def split_high(n4, off):
                slot = off % RAW
                act.wait_ge(s_raw[slot], 16 * (n4 + off // RAW + 1))
                if not (isinstance(n4, int) and n4 == 0 and off < SPLIT):
                    act.wait_ge(s_blk, ONE + n4 * RAW + (off - SPLIT + 1))
                copy(wh[:, slot, :], raw[:, slot, :]).then_inc(s_wh, 1)

            def stats(slot, rows, n, loads):
                act.wait_ge(s_x[slot], 16 * loads)
                nc.scalar.activation(junk[0:rows, :], x_t[slot][0:rows, :], ACT.Square,
                                     accum_out=xss[0:rows, slot:slot + 1]).then_inc(s_xsq, 1)
                act.wait_ge(s_xsq, n + 1)
                nc.scalar.activation(xsd[0:rows, slot:slot + 1], xss[0:rows, slot:slot + 1], ACT.Sqrt,
                                     scale=1.0 / D, bias=eps[0:rows, :]).then_inc(s_xsd, 1)

            def x_high(r, q, n):
                act.wait_ge(s_xt, n + 1)
                copy(act_h[:, 4 * q:4 * q + 4, bass.ds(META + P * r, P)],
                     XB[q].rearrange("p (k c) -> p k c", c=P)).then_inc(s_xh, 1)

            act.wait_ge(s_cst, 32)
            act.wait_ge(s_init, 6)
            eps = cst[:, C_EPS:C_EPS + 1]

            stats(1, META, 0, 1)
            stats(0, P, 1, 1)
            act.wait_ge(s_xt, 1)
            copy(act_h[:, :, 0:META], R[0][:, 0:KT * META].rearrange("p (k c) -> p k c", c=META)).then_inc(s_xh, 1)
            for r in range(ROWT):
                if r + 1 < ROWT:
                    stats((r + 1) % 2, P, r + 2, (r + 4) // 2)
                if r == 0:
                    for n in range(LEAD):
                        split_high(0, n)
                for q in range(XG):
                    x_high(r, q, 1 + XG * r + q)

            for h in range(HALVES):
                h4 = h * NBLK // RAW
                if h:
                    copy(kT[:, 0:CHUNK], kT[:, HALF:HALF + CHUNK]).then_inc(s_kd, 1)
                    copy(vT[:, 0:CHUNK], vT[:, HALF:HALF + CHUNK])
                for s in range(5):
                    split_high(h4, s + LEAD)
                product_done(act, h, 0)
                for n in range(2):
                    nc.scalar.activation(k_sq[:, half_cols(n)], R[n][:, 0:SUB], ACT.Square).then_inc(s_ksq, 1)
                split_high(h4, 5 + LEAD)
                act.wait_ge(s_kss, h + 1)
                for n, bank in enumerate((PT, PM)):
                    nc.scalar.activation(k_rs[:, half_cols(n)], bank[:, 0:SUB], ACT.Sqrt,
                                         scale=1.0 / HD, bias=eps).then_inc(s_ksd, 1)
                for s in range(6, KV_BLKS):
                    split_high(h4, s + LEAD)
                product_done(act, h, TILE_BLKS)
                copy(vT[:, CHUNK + SUB - META:CHUNK + HALF], O[:, 0:SUB]).then_inc(s_vT, 1)
                copy(vT[:, CHUNK:CHUNK + SUB - META], R[2][:, META:SUB]).then_inc(s_vT, 1)
                copy(v_meta[:, h, :], R[2][:, 0:META]).then_inc(s_vT, 1)

                def v_all_out():
                    act.wait_ge(s_vt, h + 1)
                    act.wait_ge(s_free, ONE + h * OB * ROWT)
                    copy(vm_all, R[2][0:META, 0:P]).then_inc(s_va, 1)
                    copy(v_all, S[:, :, :].rearrange("p b (c n) -> p (b c) n", c=4)).then_inc(s_va, 1)

                def k_band():
                    act.wait_ge(s_kn, h + 1)
                    for e in range(KVH):
                        for half in range(2):
                            src, dst = slice(e * HD, (e + 1) * HD), slice(half * HD, (half + 1) * HD)
                            copy(k_dup[dst, e, META:META + CHUNK + HALF], kT[src, :]).then_inc(s_kd, 1)
                            copy(k_dup[dst, e, 0:META], k_meta[src, 0, :]).then_inc(s_kd, 1)
                    act.wait_ge(s_kd, 9 * h + 8)
                    kb = kb_h[:, :, :].rearrange("p e (c n) -> p e c n", n=BAND)
                    for e in range(KVH):
                        copy(kb[:, e, :, 0:CHUNK],
                             k_dup[:, e, META:].rearrange("p (c n) -> p c n", n=CHUNK)).then_inc(s_kbh, 1)
                        copy(kb[:, e, :, CHUNK:BAND],
                             k_dup[:, e, 0:META].unsqueeze(1).to_broadcast([P, NCH + 1, META])).then_inc(s_kbh, 1)

                v_all_out()
                with act.Fori(0, PAIRS // 4) as jq:
                    def q_square(t):
                        product_done(act, h, KV_BLKS + (jq * 4 + t) * TILE_BLKS)
                        if t >= 2:
                            act.wait_ge(s_qss, h * PAIRS + jq * 4 + t - 1)
                        nc.scalar.activation(q_sq[t % 2], QB[t][:, :], ACT.Square).then_inc(s_qsq, 1)

                    def q_sqrt(t):
                        act.wait_ge(s_qss, h * PAIRS + jq * 4 + t + 1)
                        if t >= 2:
                            act.wait_ge(s_qn, QB_FREE + h * PAIRS + jq * 4 + t - 1)
                        else:
                            act.wait_ge(s_qn, QB_FREE + h * PAIRS + jq * 4)
                        nc.scalar.activation(q_rs[t % 2], (PT, PM)[t % 2][:, :], ACT.Sqrt,
                                             scale=1.0 / HD, bias=eps).then_inc(s_qsd, 1)

                    for s in range(4 * TILE_BLKS + 1):
                        if s < 4 * TILE_BLKS:
                            split_high(h4 + KV_BLKS // RAW + jq * 4, s + LEAD)
                        if s and s % 4 == 0:
                            q_square(s // 4 - 1)
                        if s > 4 and s % 4 == 1:
                            q_sqrt(s // 4 - 1)
                    q_sqrt(3)
                k_band()
                act.wait_ge(s_qn, QB_FREE + (h + 1) * PAIRS)

                with act.Fori(0, KVH) as e:
                    act.wait_ge(s_o, ONE + (h * KVH + e) * 2 * UNITS)
                    for dup in range(2):
                        copy(v_h[:, :, dup, :], v_all[:, :, bass.ds(e * HD, HD)]).then_inc(s_vh, 1)
                        for at in (0, 32):
                            copy(vm[at:at + META, dup, :], vm_all[:, bass.ds(e * HD, HD)]).then_inc(s_vh, 1)
                    with act.Fori(0, 2) as gg:
                        g = e * 2 + gg
                        G = h * GROUPS + g
                        n0 = KV_BLKS + Q_BLKS + g * G_BLKS
                        n4 = h4 + (KV_BLKS + Q_BLKS) // RAW + g * (G_BLKS // RAW)

                        def qdiag(u):
                            act.wait_ge(s_s, ONE + G * UNITS + u)
                            q = mixed[:, bass.ds(PAIRS + g * 2 + u // 2, 1),
                                      (u % 2) * 256:(u % 2) * 256 + 256].rearrange(
                                          "p a (c t) -> p (a c) t", t=CHUNK)
                            copy(qd_h[0:HD, :, 0, :], q[0:HD]).then_inc(s_qdh, 1)
                            copy(qd_h[HD:P, :, 1, :], q[HD:P]).then_inc(s_qdh, 1)

                        def exps(u):
                            act.wait_ge(s_nm, G * UNITS + u + 1)
                            sink = vec[:, bass.ds(V_SINK + g * 2 + u // 2, 1)]
                            for c in range(QUAD):
                                nc.scalar.activation(
                                    prob[:, c, :], S[:, c // 2, (c % 2) * KEYS:(c % 2 + 1) * KEYS], ACT.Exp,
                                    bias=nmax[:, c:c + 1], accum_out=den[:, c:c + 1]).then_inc(s_ex, 1)
                            nc.scalar.activation(esink[:, :], nmax[:, :], ACT.Exp, bias=sink).then_inc(s_ex, 1)

                        def p_high(u):
                            act.wait_ge(s_tp, ONE + G * UNITS + u + 1)
                            act.wait_ge(s_o, ONE + G * UNITS + u)
                            copy(pt_h[:, :], PT[:, :]).then_inc(s_ph, 1)
                            copy(pm[0:META, :], PM[0:META, :]).then_inc(s_ph, 1)
                            copy(pm[64:64 + META, :], PM[0:META, :]).then_inc(s_ph, 1)

                        def gate_exp(n, bank):
                            product_done(act, h, n0 + (0, 4, 16, 20)[n])
                            if n < 2:
                                act.wait_ge(s_oe, ONE + G * UNITS)
                            else:
                                act.wait_ge(s_me, ONE + G * 2)
                            nc.scalar.activation(gate[n], bank[:, :], ACT.Exp, scale=-1.0).then_inc(s_ge[n], 1)

                        def pv_out(jj, banks):
                            product_done(act, h, n0 + 8 + 4 * jj)
                            act.wait_ge(s_dl, ONE + G * 2)
                            for n in range(2):
                                ins = copy(pv[jj][:, half_cols(n)], banks[n][:, 0:SUB])
                            ins.then_inc(s_pve, 1)

                        def d_high(jj):
                            act.wait_ge(s_d, ONE + G * 2 + jj + 1)
                            act.wait_ge(s_mix, ONE + G * 2)
                            copy(d_h[:, jj, :], pv[jj][:, META:COLS]).then_inc(s_dh, 1)

                        def pw_high():
                            act.wait_ge(s_pw, 16 * (G + 1))
                            act.wait_ge(s_mix, ONE + G * 2)
                            copy(pw_h[:, :], pw_raw).then_inc(s_pwh, 1)

                        todo = {s: [] for s in range(G_BLKS + 1)}
                        for u in range(UNITS):
                            todo[4 * u + 1].append((qdiag, u))
                            todo[4 * u + 5].append((exps, u))
                            todo[4 * u + 9].append((p_high, u))
                        todo[2].append((pw_high,))
                        todo[4].append((gate_exp, 0, R[0]))
                        todo[8].append((gate_exp, 1, R[1]))
                        todo[12].append((pv_out, 0, (R[2], R[0])))
                        todo[16].append((pv_out, 1, (R[1], R[2])))
                        todo[16].append((d_high, 0))
                        todo[20].append((gate_exp, 2, R[0]))
                        todo[20].append((d_high, 1))
                        todo[24].append((gate_exp, 3, R[1]))
                        for s in range(G_BLKS + 1):
                            if s < G_BLKS:
                                split_high(n4, s + LEAD)
                            for f, *a in todo[s]:
                                f(*a)

                if h == 0:
                    act.wait_ge(s_blk, ONE + h * NBLK + IN_BLKS)
                    copy(act_h[:, :, 0:META], act_h[:, :, HALF:COLS].bitcast(f32)).then_inc(s_xh, 1)
                    copy(act_l[:, :, 0:META], act_l[:, :, HALF:COLS].bitcast(f32)).then_inc(s_xh, 1)

                def out_splits(nb, frames, last, turn=0):
                    def mix_high(k):
                        if k < 12:
                            pass
                        act.wait_ge(s_blk, ONE + h * NBLK + IN_BLKS + nb * KT + (k - 4 + 1) if k >= 4 else
                                    ONE + h * NBLK + IN_BLKS + nb * KT - 4 + k + 1)
                        if k < 2:
                            act.wait_ge(s_s, ONE + (h + 1) * GROUPS * UNITS)
                        elif k < 4:
                            act.wait_ge(s_o, ONE + (h + 1) * GROUPS * UNITS)
                        if k == 12:
                            act.wait_ge(s_me, ONE + (h + 1) * GROUPS * 2)
                        if k == 14:
                            act.wait_ge(s_oe, ONE + (h + 1) * GROUPS * UNITS)
                        copy(mix_h[k % 4], mixed[:, K_ORDER[k], :]).then_inc(s_mh, 1)

                    for k in range(LEAD):
                        mix_high(k)
                    for k in range(KT):
                        if not last or k < KT - LEAD:
                            split_high(h4 + IN_BLKS // RAW + nb * (KT // RAW), k + LEAD)
                        if k + LEAD < KT:
                            mix_high(k + LEAD)
                        if frames is not None:
                            if k == 4:
                                stats(frames, P, ROWT + 1 + nb, 3 + frames + turn)
                            if k >= 9 and k < 9 + XG:
                                x_high(nb, k - 9, 1 + XG * (ROWT + nb) + k - 9)

                if h == 0:
                    with act.Fori(0, 2) as i:
                        for v in range(2):
                            out_splits(i * 2 + v, v, False, i)
                else:
                    with act.Fori(0, OB - 1) as nb:
                        out_splits(nb, None, False)
                    out_splits(OB - 1, None, True)

        @block.vector
        def _(dve):
            def sub(dst, a, b):
                return nc.vector.tensor_tensor(dst, a, b, ALU.subtract)

            def split_low(n4, off):
                slot = off % RAW
                dve.wait_ge(s_wh, n4 * RAW + off + 1)
                sub(wl[:, slot, :], raw[:, slot, :], wh[:, slot, :]).then_inc(s_wl, 1)

            def norm(slot, rows, n, g_loaded):
                dve.wait_ge(s_xsd, n + 1)
                nc.vector.reciprocal(xrs[0:rows, slot:slot + 1], xsd[0:rows, slot:slot + 1]).then_inc(s_xrs, 1)
                dve.wait_ge(s_xrs, n + 1)
                dve.wait_ge(g_loaded, 16)
                nc.vector.scalar_tensor_tensor(x_t[slot][0:rows, :], x_t[slot][0:rows, :],
                                               xrs[0:rows, slot:slot + 1], g_row[0:rows, :],
                                               ALU.mult, ALU.mult).then_inc(s_xn, 1)

            def x_low(r, q, n):
                dve.wait_ge(s_xh, n + 1)
                cols = bass.ds(META + P * r, P)
                sub(act_l[:, 4 * q:4 * q + 4, cols], XB[q].rearrange("p (k c) -> p k c", c=P),
                    act_h[:, 4 * q:4 * q + 4, cols]).then_inc(s_xl, 1)

            dve.wait_ge(s_cst, 32)
            dve.wait_ge(s_init, 6)
            nc.vector.tensor_scalar(gq8[:, :], vec[:, V_GQ:V_GQ + 1], HD ** -0.5, None, ALU.mult).then_inc(s_gq, 1)
            dve.wait_ge(s_gq, 1)

            norm(1, META, 0, s_g)
            norm(0, P, 1, s_g)
            dve.wait_ge(s_xh, 1)
            sub(act_l[:, :, 0:META], R[0][:, 0:KT * META].rearrange("p (k c) -> p k c", c=META),
                act_h[:, :, 0:META]).then_inc(s_xl, 1)
            for r in range(ROWT):
                if r + 1 < ROWT:
                    norm((r + 1) % 2, P, r + 2, s_g)
                for q in range(XG):
                    x_low(r, q, 1 + XG * r + q)
                if r == 0:
                    for n in range(LEAD):
                        split_low(0, n)

            for h in range(HALVES):
                h4 = h * NBLK // RAW
                gk = vec[:, V_GK:V_GK + 1]
                for s in range(7):
                    split_low(h4, s + LEAD)
                dve.wait_ge(s_ksd, 2 * (h + 1))
                nc.vector.reciprocal(k_rs, k_rs).then_inc(s_krs, 1)
                dve.wait_ge(s_krs, h + 1)
                if h:
                    dve.wait_ge(s_kd, 9)
                nc.vector.scalar_tensor_tensor(k_meta[:, h, :], R[0][:, 0:META], gk,
                                               k_rs[:, 0:META], ALU.mult, ALU.mult)
                nc.vector.scalar_tensor_tensor(kT[:, CHUNK:CHUNK + SUB - META], R[0][:, META:SUB], gk,
                                               k_rs[:, META:SUB], ALU.mult, ALU.mult)
                nc.vector.scalar_tensor_tensor(kT[:, CHUNK + SUB - META:CHUNK + HALF], R[1][:, 0:SUB], gk,
                                               k_rs[:, SUB:COLS], ALU.mult, ALU.mult).then_inc(s_kn, 1)
                split_low(h4, 7 + LEAD)

                with dve.Fori(0, PAIRS // 4) as jq:
                    def q_norm(t):
                        n = h * PAIRS + jq * 4 + t
                        dve.wait_ge(s_qsd, n + 1)
                        nc.vector.reciprocal(q_rs[t % 2], q_rs[t % 2]).then_inc(s_qrs, 1)
                        dve.wait_ge(s_qrs, n + 1)
                        nc.vector.scalar_tensor_tensor(mixed[:, bass.ds(PAIRS + jq * 4 + t, 1), :],
                                                       QB[t][:, :].unsqueeze(1), gq8[:, :],
                                                       q_rs[t % 2].unsqueeze(1), ALU.mult, ALU.mult).then_inc(s_qn, 1)

                    for s in range(4 * TILE_BLKS + 1):
                        if s < 4 * TILE_BLKS:
                            split_low(h4 + KV_BLKS // RAW + jq * 4, s + LEAD)
                        if s > 4 and s % 4 == 2:
                            q_norm(s // 4 - 1)
                    q_norm(3)
                kb = kb_h[:, :, :].rearrange("p e (c n) -> p e c n", n=BAND)
                kl = kb_l[:, :, :].rearrange("p e (c n) -> p e c n", n=BAND)
                for e in range(KVH):
                    dve.wait_ge(s_kbh, 4 * h + 2 * e + 2)
                    sub(kl[:, e, :, 0:CHUNK], k_dup[:, e, META:].rearrange("p (c n) -> p c n", n=CHUNK),
                        kb[:, e, :, 0:CHUNK])
                    ins = sub(kl[:, e, :, CHUNK:BAND],
                              k_dup[:, e, 0:META].unsqueeze(1).to_broadcast([P, NCH + 1, META]),
                              kb[:, e, :, CHUNK:BAND])
                ins.then_inc(s_kbl, 1)

                with dve.Fori(0, KVH) as e:
                    dve.wait_ge(s_vh, 6 * (h * KVH + e + 1))
                    for dup in range(2):
                        sub(v_l[:, :, dup, :], v_all[:, :, bass.ds(e * HD, HD)], v_h[:, :, dup, :])
                        ins = sub(vm[64:64 + META, dup, :], vm_all[:, bass.ds(e * HD, HD)], vm[0:META, dup, :])
                    ins.then_inc(s_vl, 1)
                    with dve.Fori(0, 2) as gg:
                        g = e * 2 + gg
                        G = h * GROUPS + g
                        n4 = h4 + (KV_BLKS + Q_BLKS) // RAW + g * (G_BLKS // RAW)

                        def qdiag(u):
                            dve.wait_ge(s_qdh, (G * UNITS + u + 1) * 2)
                            q = mixed[:, bass.ds(PAIRS + g * 2 + u // 2, 1),
                                      (u % 2) * 256:(u % 2) * 256 + 256].rearrange(
                                          "p a (c t) -> p (a c) t", t=CHUNK)
                            sub(qd_l[0:HD, :, 0, :], q[0:HD], qd_h[0:HD, :, 0, :])
                            sub(qd_l[HD:P, :, 1, :], q[HD:P], qd_h[HD:P, :, 1, :]).then_inc(s_qdl, 1)

                        def row_max(u):
                            dve.wait_ge(s_s, ONE + G * UNITS + u + 1)
                            nc.vector.tensor_reduce(
                                smax[:, :].rearrange("p (b c) -> p b c", b=2),
                                S[:, :, 0:2 * KEYS].rearrange("p b (c k) -> p b c k", c=2),
                                AX.X, ALU.max).then_inc(s_mx, 1)
                            dve.wait_ge(s_mx, G * UNITS + u + 1)
                            sink = vec[:, bass.ds(V_SINK + g * 2 + u // 2, 1)]
                            nc.vector.tensor_scalar(nmax[:, :], smax[:, :], sink, -1.0,
                                                    ALU.max, ALU.mult).then_inc(s_nm, 1)

                        def normalise(u):
                            n = G * UNITS + u
                            dve.wait_ge(s_ex, ONE + (n + 1) * (QUAD + 1))
                            nc.vector.tensor_tensor(dtot[:, :], den[:, :], esink[:, :], ALU.add).then_inc(s_dt, 1)
                            dve.wait_ge(s_dt, n + 1)
                            nc.vector.reciprocal(rden[:, :], dtot[:, :]).then_inc(s_rd, 1)
                            dve.wait_ge(s_rd, n + 1)
                            dve.wait_ge(s_tp, ONE + n)
                            r = rden[:, :].unsqueeze(2)
                            pc = pn.rearrange("p (c k) -> p c k", c=QUAD)
                            nc.vector.tensor_tensor(pc[:, :, 0:CHUNK], prob[:, :, 0:CHUNK],
                                                    r.to_broadcast([P, QUAD, CHUNK]), ALU.mult)
                            nc.vector.tensor_tensor(pc[:, :, CHUNK:P], prob[:, :, BAND:KEYS],
                                                    r.to_broadcast([P, QUAD, CHUNK]), ALU.mult)
                            nc.vector.tensor_tensor(pnm.rearrange("p (c k) -> p c k", c=QUAD),
                                                    prob[:, :, CHUNK:BAND],
                                                    r.to_broadcast([P, QUAD, META]), ALU.mult).then_inc(s_pn, 1)

                        def p_low(u):
                            dve.wait_ge(s_ph, (G * UNITS + u + 1) * 3)
                            sub(pt_l[:, :], PT[:, :], pt_h[:, :])
                            sub(pm[32:32 + META, :], PM[0:META, :], pm[0:META, :]).then_inc(s_pl, 1)

                        def o_out(u):
                            dve.wait_ge(s_o, ONE + G * UNITS + u + 1)
                            dve.wait_ge(s_gt[u // 2], ONE + G + 1)
                            cols = slice((u % 2) * 256, (u % 2) * 256 + 256)
                            o = O[:, :].rearrange("p (c e t) -> p c e t", e=2, t=CHUNK)
                            gt = gate[u // 2][:, cols].rearrange("p (c t) -> p c t", t=CHUNK)
                            dst = mixed[:, bass.ds(PAIRS + g * 2 + u // 2, 1), cols].rearrange(
                                "p a (c t) -> p (a c) t", t=CHUNK)
                            nc.vector.tensor_tensor(dst[0:HD], o[0:HD, :, 0, :], gt[0:HD], ALU.mult)
                            nc.vector.tensor_tensor(dst[HD:P], o[HD:P, :, 1, :], gt[HD:P],
                                                    ALU.mult).then_inc(s_oe, 1)

                        def silu(n, bank):
                            dve.wait_ge(s_ge[n], G + 1)
                            nc.vector.tensor_scalar(gate[n], gate[n], 1.0, None, ALU.add).then_inc(s_ga, 1)
                            dve.wait_ge(s_ga, G * 4 + n + 1)
                            nc.vector.reciprocal(gate[n], gate[n]).then_inc(s_gr, 1)
                            dve.wait_ge(s_gr, G * 4 + n + 1)
                            nc.vector.tensor_tensor(gate[n], bank[:, :], gate[n], ALU.mult).then_inc(s_gt[n], 1)

                        def pooled(jj):
                            dve.wait_ge(s_sum, G * 2 + jj + 1)
                            nc.vector.scalar_tensor_tensor(
                                pv[jj][:, META:COLS], psum_w[0][:, META:COLS],
                                cst[:, bass.ds(C_INVW + g, 1)], pv[jj][:, META:COLS],
                                ALU.mult, ALU.subtract).then_inc(s_d, 1)

                        def d_low(jj):
                            dve.wait_ge(s_dh, G * 2 + jj + 1)
                            sub(d_l[:, jj, :], pv[jj][:, META:COLS], d_h[:, jj, :]).then_inc(s_dl, 1)

                        def pw_low():
                            dve.wait_ge(s_pwh, G + 1)
                            sub(pw_l[:, :], pw_raw, pw_h[:, :]).then_inc(s_pwl, 1)

                        def mix_out(jj, bank):
                            dve.wait_ge(s_mix, ONE + G * 2 + jj + 1)
                            dve.wait_ge(s_gt[2 + jj], ONE + G + 1)
                            nc.vector.scalar_tensor_tensor(
                                mixed[:, bass.ds(g * 2 + jj, 1), :], bank[:, :].unsqueeze(1),
                                vec[:, bass.ds(V_SCALE + g * 2 + jj, 1)], gate[2 + jj].unsqueeze(1),
                                ALU.mult, ALU.mult).then_inc(s_me, 1)

                        todo = {s: [] for s in range(G_BLKS + 1)}
                        for u in range(UNITS):
                            todo[4 * u + 1].append((qdiag, u))
                            todo[4 * u + 4].append((row_max, u))
                            todo[4 * u + 6].append((normalise, u))
                            todo[4 * u + 9].append((p_low, u))
                            todo[4 * u + 11].append((o_out, u))
                        todo[2].append((pw_low,))
                        todo[5].append((silu, 0, R[0]))
                        todo[9].append((silu, 1, R[1]))
                        todo[15].append((pooled, 0))
                        todo[17].append((d_low, 0))
                        todo[19].append((pooled, 1))
                        todo[21].append((d_low, 1))
                        todo[21].append((silu, 2, R[0]))
                        todo[24].append((silu, 3, R[1]))
                        todo[24].append((mix_out, 0, PT))
                        todo[24].append((mix_out, 1, O))
                        for s in range(G_BLKS + 1):
                            if s < G_BLKS:
                                split_low(n4, s + LEAD)
                            for f, *a in todo[s]:
                                f(*a)

                def out_splits(nb, frames, last, turn=0):
                    def mix_low(k):
                        dve.wait_ge(s_mh, (h * OB + nb) * KT + k + 1)
                        sub(mix_l[k % 4], mixed[:, K_ORDER[k], :], mix_h[k % 4]).then_inc(s_ml, 1)

                    for k in range(LEAD):
                        mix_low(k)
                    for k in range(KT):
                        if not last or k < KT - LEAD:
                            split_low(h4 + IN_BLKS // RAW + nb * (KT // RAW), k + LEAD)
                        if k + LEAD < KT:
                            mix_low(k + LEAD)
                        if frames is not None:
                            if k == 5:
                                norm(frames, P, ROWT + 1 + nb, s_g2)
                            if k >= 9 and k < 9 + XG:
                                x_low(nb, k - 9, 2 + XG * (ROWT + nb) + 1 + k - 9)
                    for r in range(ROWT):
                        if r < ROWT - 1:
                            dve.wait_ge(s_y, (h * OB + nb) * (ROWT - 1) + r + 1)
                        else:
                            dve.wait_ge(s_blk, ONE + h * NBLK + IN_BLKS + (nb + 1) * KT)
                        dve.wait_ge(s_res[r], 16 * (h * OB + nb + 1))
                        nc.vector.tensor_tensor(y[r], YB[r][:, :], y[r], ALU.add).then_inc(s_ye, 1)

                if h == 0:
                    with dve.Fori(0, 2) as i:
                        for v in range(2):
                            out_splits(i * 2 + v, v, False, i)
                else:
                    with dve.Fori(0, OB - 1) as nb:
                        out_splits(nb, None, False)
                    out_splits(OB - 1, None, True)

        @block.tensor
        def _(pe):
            mm = nc.tensor.matmul

            def tile(h, n, banks, cols, events=None, slot0=0):
                for b in range(TILE_BLKS):
                    pe.wait_ge(s_wl, ONE + h * NBLK + n + b + 1)
                    for kk in range(4):
                        k = 4 * b + kk
                        w = slice(kk * P, (kk + 1) * P)
                        for bank, c in zip(banks, cols):
                            o = bank[:, 0:c.stop - c.start]
                            mm(o, wh[:, b, w], act_h[:, k, c], start=(k == 0), stop=False)
                            mm(o, wh[:, b, w], act_l[:, k, c], start=False, stop=False)
                        for bank, c in zip(banks, cols):
                            o = bank[:, 0:c.stop - c.start]
                            last = mm(o, wl[:, b, w], act_h[:, k, c], start=False, stop=(k == KT - 1))
                    last.then_inc(s_blk, 1)
                    if events:
                        events(slot0 + b)

            both = (half_cols(0), half_cols(1))
            own = (slice(META, COLS),)

            def x_group(slot, q):
                for kk in range(4):
                    k = 4 * q + kk
                    last = nc.tensor.transpose(XB[q][:, kk * P:(kk + 1) * P],
                                               x_t[slot][:, k * P:(k + 1) * P], ident)
                last.then_inc(s_xt, 1)

            pe.wait_ge(s_cst, 32)
            pe.wait_ge(s_init, 6)

            pe.wait_ge(s_xn, 1)
            for k in range(KT):
                last = nc.tensor.transpose(R[0][:, k * META:(k + 1) * META],
                                           x_t[1][0:META, k * P:(k + 1) * P], ident[0:META, 0:META])
            last.then_inc(s_xt, 1)
            for r in range(ROWT):
                pe.wait_ge(s_xn, r + 2)
                for q in range(XG):
                    if r:
                        pe.wait_ge(s_xl, 1 + XG * (r - 1) + q + 1)
                    x_group(r % 2, q)

            for h in range(HALVES):
                pe.wait_ge(s_xl, 1 + XG * ROWT * (h + 1))
                if h:
                    pe.wait_ge(s_xh, 3 + XG * ROWT * 2)
                    pe.wait_ge(s_ye, ONE + OB * ROWT - 2)

                def k_squares(s):
                    if s == TILE_BLKS:
                        pe.wait_ge(s_ksq, 2 * (h + 1))
                        for n, bank in enumerate((PT, PM)):
                            last = mm(bank[:, 0:SUB], blkones, k_sq[:, half_cols(n)], start=True, stop=True)
                        last.then_inc(s_kss, 1)

                tile(h, 0, (R[0], R[1]), both)
                if h:
                    pe.wait_ge(s_ye, ONE + OB * ROWT)
                tile(h, TILE_BLKS, (R[2], O), both, events=k_squares, slot0=TILE_BLKS)

                def v_windows():
                    pe.wait_ge(s_vT, 3 * (h + 1))
                    nc.tensor.transpose(R[2][0:META, 0:P], v_meta[:, 0, :], ident)
                    for c in range(NCH):
                        last = nc.tensor.transpose(S[:, c // 4, (c % 4) * P:(c % 4 + 1) * P],
                                                   vT[:, c * CHUNK:c * CHUNK + P], ident)
                    last.then_inc(s_vt, 1)

                v_windows()
                with pe.Fori(0, PAIRS // 4) as jq:
                    q0 = h * PAIRS + jq * 4

                    def sum_squares(t):
                        pe.wait_ge(s_qsq, q0 + t + 1)
                        if t >= 2:
                            pe.wait_ge(s_qsd, q0 + t - 1)
                        mm((PT, PM)[t % 2][:, :], blkones, q_sq[t % 2], start=True, stop=True).then_inc(s_qss, 1)

                    def events(s):
                        if s > 1 and s % 4 == 0:
                            sum_squares(s // 4 - 1)

                    for t in range(4):
                        pe.wait_ge(s_qn, QB_FREE + q0 + t - 3)
                        if t == 0:
                            pe.wait_ge(s_vT, 3 * (h + 1))
                        elif t == 1:
                            pe.wait_ge(s_va, 2 * (h + 1))
                        elif t == 2:
                            pe.wait_ge(s_kn, h + 1)
                        tile(h, KV_BLKS + (jq * 4 + t) * TILE_BLKS, (QB[t],), own, events=events, slot0=4 * t)
                    sum_squares(3)

                with pe.Fori(0, KVH) as e:
                    with pe.Fori(0, 2) as gg:
                        g = e * 2 + gg
                        G = h * GROUPS + g

                        def scores(u):
                            pe.wait_ge(s_qdl, G * UNITS + u + 1)
                            pe.wait_ge(s_ex, ONE + (G * UNITS + u) * (QUAD + 1))
                            pe.wait_ge(s_kbl, ONE + h + 1)
                            for c in range(QUAD):
                                ch = (u % 2) * QUAD + c
                                o = S[:, c // 2, (c % 2) * KEYS:(c % 2 + 1) * KEYS]
                                keys_h = kb_h[:, bass.ds(e, 1), ch * BAND:ch * BAND + KEYS].rearrange("p a k -> p (a k)")
                                keys_l = kb_l[:, bass.ds(e, 1), ch * BAND:ch * BAND + KEYS].rearrange("p a k -> p (a k)")
                                qh = qd_h[:, c, :, :].rearrange("p a t -> p (a t)")
                                ql = qd_l[:, c, :, :].rearrange("p a t -> p (a t)")
                                masked = h == 0 and ch == 0
                                mm(o, qh, keys_h, start=True, stop=False)
                                mm(o, qh, keys_l, start=False, stop=False)
                                last = mm(o, ql, keys_h, start=False, stop=not masked)
                                if masked:
                                    last = mm(o, ones_row, cst[0:1, C_MASK:C_MASK + KEYS],
                                              start=False, stop=True)
                            last.then_inc(s_s, 1)

                        def transposes(u):
                            n = G * UNITS + u
                            pe.wait_ge(s_pn, n + 1)
                            pe.wait_ge(s_pl, ONE + n)
                            pe.wait_ge(s_me, ONE + G * 2)
                            for c in range(QUAD):
                                nc.tensor.transpose(PT[:, c * P:(c + 1) * P], pn[:, c * P:(c + 1) * P], ident)
                            for c in range(QUAD):
                                last = nc.tensor.transpose(PM[0:META, c * P:(c + 1) * P],
                                                           pnm[:, c * META:(c + 1) * META], ident)
                            last.then_inc(s_tp, 1)

                        def values(u):
                            n = G * UNITS + u
                            pe.wait_ge(s_pl, ONE + n + 1)
                            pe.wait_ge(s_vl, h * KVH + e + 1)
                            pe.wait_ge(s_oe, ONE + n)
                            mm(O[:, :], vm[:, :, :].rearrange("p a d -> p (a d)"), pm[:, :], start=True, stop=False)
                            for c in range(QUAD):
                                ch = (u % 2) * QUAD + c
                                cs = slice(c * P, (c + 1) * P)
                                vh = v_h[:, ch, :, :].rearrange("p a d -> p (a d)")
                                vl = v_l[:, ch, :, :].rearrange("p a d -> p (a d)")
                                mm(O[:, cs], vh, pt_h[:, cs], start=False, stop=False)
                                mm(O[:, cs], vh, pt_l[:, cs], start=False, stop=False)
                                last = mm(O[:, cs], vl, pt_h[:, cs], start=False, stop=(c == QUAD - 1))
                            last.then_inc(s_o, 1)

                        when = {}
                        for u in range(UNITS):
                            when.setdefault(4 * u + 3, []).append((scores, u))
                            when.setdefault(4 * u + 8, []).append((transposes, u))
                            when.setdefault(4 * u + 10, []).append((values, u))

                        def events(s):
                            for f, u in when.get(s, ()):
                                f(u)

                        n0 = KV_BLKS + Q_BLKS + g * G_BLKS
                        pe.wait_ge(s_qn, QB_FREE + h * PAIRS + 7)
                        pe.wait_ge(s_gt[2], ONE + G)
                        tile(h, n0, (R[0],), own, events=events, slot0=0)
                        pe.wait_ge(s_qn, QB_FREE + h * PAIRS + 8)
                        pe.wait_ge(s_gt[3], ONE + G)
                        tile(h, n0 + 4, (R[1],), own, events=events, slot0=4)
                        pe.wait_ge(s_gt[0], ONE + G + 1)
                        pe.wait_ge(s_pve, ONE + G * 2)
                        tile(h, n0 + 8, (R[2], R[0]), both, events=events, slot0=8)
                        pe.wait_ge(s_gt[1], ONE + G + 1)
                        pe.wait_ge(s_pve, ONE + G * 2 + 1)
                        tile(h, n0 + 12, (R[1], R[2]), both, events=events, slot0=12)
                        tile(h, n0 + 16, (R[0],), own, events=events, slot0=16)
                        pe.wait_ge(s_pve, ONE + G * 2 + 2)
                        tile(h, n0 + 20, (R[1],), own, events=events, slot0=20)
                        pe.wait_ge(s_dl, ONE + G * 2 + 2)
                        pe.wait_ge(s_pwl, ONE + G + 1)
                        for jj, bank in enumerate((PT, O)):
                            if jj == 0:
                                pe.wait_ge(s_pl, ONE + (G + 1) * UNITS)
                            else:
                                pe.wait_ge(s_oe, ONE + (G + 1) * UNITS)
                            for a in range(2):
                                w = slice(a * 256 + jj * P, a * 256 + (jj + 1) * P)
                                mm(bank[:, :], pw_h[:, w], d_h[:, a, :], start=(a == 0), stop=False)
                                mm(bank[:, :], pw_h[:, w], d_l[:, a, :], start=False, stop=False)
                                last = mm(bank[:, :], pw_l[:, w], d_h[:, a, :], start=False, stop=(a == 1))
                            last.then_inc(s_mix, 1)

                def project(nb, frames):
                    pe.wait_ge(s_gt[2], ONE + (h + 1) * GROUPS)
                    pe.wait_ge(s_gt[3], ONE + (h + 1) * GROUPS)
                    for k in range(KT):
                        pe.wait_ge(s_ml, (h * OB + nb) * KT + k + 1)
                        pe.wait_ge(s_wl, ONE + h * NBLK + IN_BLKS + nb * KT + k + 1)
                        for r in range(ROWT):
                            if k == 0:
                                pe.wait_ge(s_ye, ONE + (h * OB + nb) * ROWT)
                                if r == ROWT - 1:
                                    pe.wait_ge(s_me, ONE + (h + 1) * GROUPS * 2)
                            c = slice(r * P, (r + 1) * P)
                            mh, ml = mix_h[k % 4][:, c], mix_l[k % 4][:, c]
                            mm(YB[r][:, :], mh, wh[:, k % SPLIT, :], start=(k == 0), stop=False)
                            mm(YB[r][:, :], mh, wl[:, k % SPLIT, :], start=False, stop=False)
                            last = mm(YB[r][:, :], ml, wh[:, k % SPLIT, :], start=False, stop=(k == KT - 1))
                            if k == KT - 1 and r < ROWT - 1:
                                last.then_inc(s_y, 1)
                        last.then_inc(s_blk, 1)
                        if frames is not None and 7 <= k < 7 + XG:
                            q = k - 7
                            if q == 0:
                                pe.wait_ge(s_xn, ROWT + 2 + nb)
                                pe.wait_ge(s_me, ONE + (h + 1) * GROUPS * 2)
                            pe.wait_ge(s_xl, 1 + XG * (ROWT + nb - 1) + q + 1)
                            x_group(frames, q)

                if h == 0:
                    with pe.Fori(0, 2) as i:
                        for v in range(2):
                            project(i * 2 + v, v)
                else:
                    with pe.Fori(0, OB) as nb:
                        project(nb, None)



def _block_layout(w_in):
    import numpy as np
    tiles = [24, 25] + list(range(16, 24))
    for g in range(GROUPS):
        tiles += [26 + 2 * g, 27 + 2 * g, 2 * g, 2 * g + 1, 8 + 2 * g, 9 + 2 * g]
    w = w_in.reshape(4, 4, P, -1, P)
    w = w[:, :, :, tiles, :].transpose(3, 0, 2, 1, 4)
    return np.ascontiguousarray(w).reshape(len(tiles) * 4, P, BLK)


def _constants():
    import numpy as np
    c = np.zeros((P, C_N), np.float32)
    c[:, C_ID:C_ID + P] = np.eye(P)
    c[:, C_BLK:C_BLK + P] = np.kron(np.eye(2), np.ones((HD, HD)))
    c[:, C_ONE:C_ONE + P] = 1.0
    c[:, C_MASK:C_MASK + CHUNK] = MASKED
    for g in range(GROUPS):
        c[:, C_INVW + g] = 0.5 ** (g + 1)
    c[:, C_EPS] = EPS
    return c


def kernel(x, meta_tokens, norm_g, w_in, pool_w, pool_scale, q_norm_g, k_norm_g, sinks, w_out):
    import numpy as np
    import concourse.bacc as bacc
    from concourse.bass_utils import run_bass_kernel_spmd

    a = lambda t: np.asarray(t)
    vecs = np.concatenate([
        a(pool_scale)[0].reshape(PAIRS, P).T,
        np.repeat(a(sinks)[0].reshape(PAIRS, 2).T, HD, axis=0),
        np.tile(a(q_norm_g)[0], 2)[:, None],
        np.tile(a(k_norm_g)[0], 2)[:, None]], axis=1)
    arrays = {
        "xcat": np.concatenate([a(meta_tokens), a(x)[0]], axis=0),
        "norm_g_in": a(norm_g)[0],
        "w_in_blocks": _block_layout(a(w_in)[0]),
        "w_out_in": a(w_out)[0],
        "pool_w_in": a(pool_w)[0],
        "vecs": vecs,
        "consts": _constants(),
    }
    arrays = {n: np.ascontiguousarray(v) for n, v in arrays.items()}
    nc = bacc.Bacc("TRN2", target_bir_lowering=False, num_devices=1)
    args = [nc.dram_tensor(n, v.shape, mybir.dt.from_np(v.dtype), kind="ExternalInput").ap()
            for n, v in arrays.items()]
    out = nc.dram_tensor("out", (SEQ, D), mybir.dt.float32, kind="ExternalOutput").ap()
    hymba_layer(nc, *args, out)
    got = run_bass_kernel_spmd(nc, [arrays], core_ids=[0]).results[0]["out"]
    return np.asarray(got).reshape(1, SEQ, D)
```

```python
from contextlib import ExitStack

import concourse.bass as bass
from concourse import mybir

P = 128
D = 2048
KT = D // P
META = 16
SEQ = 1024
HALF = 512
HALVES = SEQ // HALF
COLS = META + HALF
SUB = COLS // 2
SPANS = ((slice(0, SUB), slice(SUB, COLS)), (slice(META, COLS),))
SPANS_BY = (0, 2, 3)
CHUNK = 64
NCH = HALF // CHUNK
HD = 64
PAIRS = 8
KVH = 2
GROUPS = 4
QUAD = 4
BAND = META + CHUNK
KEYS = BAND + CHUNK
EPS = 1e-6
MASKED = -1e30
ONE = 1
QB_FREE = 4
YB_FREE = 4

BLK = 512
TILE_BLKS = 4
RAW = 4
SPLIT = 4
LEAD = 3
KV_BLKS = 2 * TILE_BLKS
Q_BLKS = PAIRS * TILE_BLKS
G_BLKS = 6 * TILE_BLKS
IN_BLKS = KV_BLKS + Q_BLKS + GROUPS * G_BLKS
OB = D // BLK
OUT_BLKS = OB * KT
NBLK = IN_BLKS + OUT_BLKS
ROWT = HALF // P
XG = 4
X_LOAD, RES_LOAD = 6, 10
X_AT = (10, 9)
K_ORDER = [0, 1, 2, 3, 4, 5, 8, 9, 10, 11, 12, 13, 6, 7, 14, 15]
UNITS = 4

FIRST_SPLITS = {2: 2, 5: 3, 7: 4, 11: 5, 15: 6}

C_ID, C_BLK, C_MASK = 0, 128, 256
C_INVW = C_MASK + KEYS
C_EPS = C_INVW + GROUPS
C_N = C_EPS + 1
V_SCALE, V_SINK, V_GQ, V_GK, V_G = 0, 8, 16, 17, 18
V_N = V_G + KT
V_OUT = (3, 4)


def hymba_layer(nc, xcat, norm_g, w_in, w_out, pool_w, vecs, consts, out):
    f32, f32r, bf16 = mybir.dt.float32, mybir.dt.float32r, mybir.dt.bfloat16
    ACT = mybir.ActivationFunctionType
    ALU = mybir.AluOpType
    AX = mybir.AxisListType

    ctx = ExitStack()
    with ctx:
        def sb(name, shape, dt=f32):
            return ctx.enter_context(nc.sbuf_tensor(name, shape, dt))

        def sem(name):
            return ctx.enter_context(nc.semaphore(name))

        act_h = sb("act_h", [P, KT, COLS], f32r)
        act_l = sb("act_l", [P, KT, COLS], f32r)
        mixed = sb("mixed", [P, KT, HALF])
        raw = sb("raw", [P, RAW, BLK])
        wh = sb("wh", [P, SPLIT, BLK], f32r)
        wl = sb("wl", [P, SPLIT, BLK], f32r)
        kT = sb("kT", [P, CHUNK + HALF])
        vT = sb("vT", [P, CHUNK + HALF])
        k_meta = sb("k_meta", [P, META])
        v_meta = sb("v_meta", [P, META])
        pv_last = sb("pv_last", [P, 2 * GROUPS, META])
        cst = sb("cst", [P, C_N])
        vec = sb("vec", [P, V_N])
        gq8 = sb("gq8", [P, 1])
        junk = sb("junk", [P, D], bf16)
        xss = sb("xss", [P, 5])
        xsd = sb("xsd", [P, 5])
        xrs = sb("xrs", [P, 5])
        band_h = sb("band_h", [P, KVH, (NCH + 1) * BAND], f32r)
        band_x = sb("band_x", [P, KVH, (NCH + 1) * BAND], f32r)
        v_s = sb("v_s", [P, NCH, 2, HD], f32r)
        mix_x = sb("mix_x", [P, 2, BLK], f32r)
        vm = sb("vm", [96, 2, HD], f32r)
        pm = sb("pm", [96, QUAD * P], f32r)
        qs = sb("qs", [P, QUAD, 2, CHUNK], f32r)
        o_part = sb("o_part", [HD, BLK])
        pt = sb("pt", [P, QUAD, 2, P], f32r)
        d_h = sb("d_h", [P, 2, HALF], f32r)
        d_l = sb("d_l", [P, 2, HALF], f32r)
        pw_h = sb("pw_h", [P, BLK], f32r)
        pw_l = sb("pw_l", [P, BLK], f32r)
        pnm = sb("pnm", [P, QUAD, P // QUAD])
        smax = sb("smax", [P, QUAD])
        nmax = sb("nmax", [P, QUAD])
        den = sb("den", [P, QUAD])
        esink = sb("esink", [P, QUAD])
        dtot = sb("dtot", [P, QUAD])
        rden = sb("rden", [P, QUAD])

        scr = sb("scr", [P, 7168])
        x_t = [scr[:, 0:D], scr[:, D:2 * D]]
        x_first = [mixed[:, 4 * r:4 * r + 4, :].rearrange("p k c -> p (k c)") for r in range(ROWT)]
        x_meta = x_t[1][0:META, :]
        meta_sq = x_t[0][0:META, :]
        meta_g = scr[:, 0:KT * META].rearrange("p (k c) -> p k c", c=META)
        g_row = scr[:, 2 * D:3 * D]
        res2 = sb("res2", [P, 2, BLK])
        y = [scr[:, 3 * D:3 * D + BLK], scr[:, 3 * D + BLK:3 * D + 2 * BLK], res2[:, 0, :], res2[:, 1, :]]
        mix_h = [band_h[:, 0, 0:BLK], band_h[:, 1, 0:BLK],
                 v_s[:, 0:4, :, :].rearrange("p c a d -> p (c a d)"),
                 v_s[:, 4:8, :, :].rearrange("p c a d -> p (c a d)")]
        mix_l = [band_x[:, 0, 0:BLK], band_x[:, 1, 0:BLK], mix_x[:, 0, :], mix_x[:, 1, :]]
        k_sq, k_rs = scr[:, 0:COLS], scr[:, COLS:2 * COLS]
        q_sq = [scr[:, 1056:1568], scr[:, 1568:2080]]
        q_rs = [scr[:, 2080:2592], scr[:, 2592:3104]]
        k_sqh = d_h[:, :, :].rearrange("p j c -> p (j c)")[:, 0:COLS]
        k_sql = d_l[:, :, :].rearrange("p j c -> p (j c)")[:, 0:COLS]
        q_sqh = [d_h[:, 0, :], d_h[:, 1, :]]
        q_sql = [d_l[:, 0, :], d_l[:, 1, :]]
        ones_r = pw_h[:, 0:P]
        prob = scr[:, 0:QUAD * KEYS].rearrange("p (c k) -> p c k", c=QUAD)
        pn = scr[:, 576:1088]
        gate = [scr[:, 1088 + HALF * n:1088 + HALF * (n + 1)] for n in range(4)]
        pv = [scr[:, 3136:3664], scr[:, 3664:4192]]
        v_all = scr[:, 4192:5216].rearrange("p (c n) -> p c n", c=NCH)
        psum_w = [scr[:, 5216:5744], scr[:, 5744:6272]]
        pw_raw = scr[:, 6272:6784]
        vm_all = scr[0:META, 6784:6912]
        o_sum = scr[:, 6912:7168]

        R = [ctx.enter_context(nc.psum_tensor(f"R{i}", [P, BLK], f32)) for i in range(3)]
        S = ctx.enter_context(nc.psum_tensor("S", [P, 2, BLK], f32))
        PT = ctx.enter_context(nc.psum_tensor("PT", [P, BLK], f32))
        OP = ctx.enter_context(nc.psum_tensor("OP", [P, 2, BLK], f32))
        O, PM = OP[:, 0, :], OP[:, 1, :]
        KB, VB = ((R[0], R[1]), (R[1],)), ((R[2], O), (R[2],))
        PVB = (((R[2], R[0]), (R[1], R[2])), ((R[2],), (R[1],)))
        OV = OP[:, :, :].rearrange("p b (c s n) -> p (b c) s n", c=2, s=2)
        FB = [S[:, 0, :], S[:, 1, :], PT[:, :], PM]
        QB = [R[0], O, R[1], R[2]]
        YB = [R[0][:, :], S[:, 0, :], S[:, 1, :], O]
        XB = [R[1][:, :], R[2][:, :], PT[:, :], PM]

        ident = cst[:, C_ID:C_ID + P]

        s_cst = sem("s_cst")
        s_g = sem("s_g")
        s_xf = [sem(f"s_xf{r}") for r in range(ROWT + 1)]
        s_xg = sem("s_xg")
        s_x = [sem(f"s_x{i}") for i in range(2)]
        s_raw = [sem(f"s_raw{i}") for i in range(RAW)]
        s_pw = sem("s_pw")
        s_res = [sem(f"s_res{i}") for i in range(ROWT)]
        s_out = [sem(f"s_out{i}") for i in range(ROWT)]
        s_last = sem("s_last")
        s_free = sem("s_free")
        s_init = sem("s_init")
        s_gq = sem("s_gq")
        s_ones = sem("s_ones")
        s_table = sem("s_table")
        s_wh = sem("s_wh")
        s_wl = sem("s_wl")
        s_blk = sem("s_blk")
        s_xsq = sem("s_xsq")
        s_xmm = sem("s_xmm")
        s_xm = sem("s_xm")
        s_xsd = sem("s_xsd")
        s_xrs = sem("s_xrs")
        s_xn = sem("s_xn")
        s_xt = sem("s_xt")
        s_xh = sem("s_xh")
        s_xl = sem("s_xl")
        s_ksq = sem("s_ksq")
        s_ksl = sem("s_ksl")
        s_kss = sem("s_kss")
        s_ksd = sem("s_ksd")
        s_krs = sem("s_krs")
        s_kn = sem("s_kn")
        s_kd = sem("s_kd")
        s_kbh = sem("s_kbh")
        s_kbl = sem("s_kbl")
        s_vT = sem("s_vT")
        s_vt = sem("s_vt")
        s_va = sem("s_va")
        s_vh = sem("s_vh")
        s_vl = sem("s_vl")
        s_qsq = sem("s_qsq")
        s_qsl = sem("s_qsl")
        s_qss = sem("s_qss")
        s_qsd = sem("s_qsd")
        s_qrs = sem("s_qrs")
        s_qn = sem("s_qn")
        s_quh = sem("s_quh")
        s_qul = sem("s_qul")
        s_s = sem("s_s")
        s_mx = sem("s_mx")
        s_nm = sem("s_nm")
        s_ex = sem("s_ex")
        s_dt = sem("s_dt")
        s_rd = sem("s_rd")
        s_pn = sem("s_pn")
        s_tp = sem("s_tp")
        s_ph = sem("s_ph")
        s_pl = sem("s_pl")
        s_o = sem("s_o")
        s_ol = sem("s_ol")
        s_oa = sem("s_oa")
        s_oe = sem("s_oe")
        s_ge = [sem(f"s_ge{n}") for n in range(4)]
        s_ga = sem("s_ga")
        s_gr = sem("s_gr")
        s_gt = [sem(f"s_gt{n}") for n in range(4)]
        s_pve = sem("s_pve")
        s_add = sem("s_add")
        s_sum = sem("s_sum")
        s_d = sem("s_d")
        s_dh = sem("s_dh")
        s_dl = sem("s_dl")
        s_pwh = sem("s_pwh")
        s_pwl = sem("s_pwl")
        s_mix = sem("s_mix")
        s_me = sem("s_me")
        s_mh = sem("s_mh")
        s_ml = sem("s_ml")
        s_y = sem("s_y")
        s_ye = sem("s_ye")

        from_one = [s_me, s_wl, s_pwl, s_d, s_blk, s_kbl, s_o, s_s, s_oe, s_dl, s_mix, s_tp,
                    s_ex, s_pl, s_pve, *s_gt, s_free]

        block = ctx.enter_context(nc.Block())

        def product_done(eng, h, n):
            eng.wait_ge(s_blk, ONE + h * NBLK + n + TILE_BLKS)

        def span_banks(h, banks):
            return [(bank[:, 0:c.stop - c.start], c) for bank, c in zip(banks, SPANS[h])]

        def own_part(bank, c):
            lo = max(c.start, META)
            return bank[:, lo - c.start:], slice(lo - META, c.stop - META)

        @block.sync
        def _(sp):
            def load_block(n, slot, src, free=True):
                if free:
                    sp.wait_ge(s_wl, ONE + n - RAW + 1)
                sp.dma_start(raw[:, slot, :], src).then_inc(s_raw[slot], 16)

            sp.dma_start(x_meta, xcat[0:META, :]).then_inc(s_xf[ROWT], 16)
            sp.dma_start(x_first[0], xcat[META:META + P, :]).then_inc(s_xf[0], 16)
            sp.dma_start(cst[:, :], consts).then_inc(s_cst, 16)
            sp.dma_start(vec[:, :], vecs).then_inc(s_cst, 16)
            for r in range(1, ROWT):
                sp.dma_start(x_first[r], xcat[META + P * r:META + P * (r + 1), :]).then_inc(s_xf[r], 16)
            for n in range(RAW):
                load_block(n, n, w_in[n, :, :], free=False)

            for h in range(HALVES):
                h0 = h * NBLK
                for n in range(RAW if h == 0 else 0, KV_BLKS):
                    load_block(h0 + n, n % RAW, w_in[n, :, :])
                with sp.Fori(0, PAIRS) as j:
                    for b in range(TILE_BLKS):
                        n = KV_BLKS + j * TILE_BLKS + b
                        load_block(h0 + n, b % RAW, w_in[n, :, :])
                sp.wait_ge(s_free, ONE + h * OB * ROWT)
                with sp.Fori(0, GROUPS) as g:
                    sp.wait_ge(s_pwl, ONE + h * GROUPS + g)
                    sp.dma_start(pw_raw.rearrange("p (a c) -> p a c", a=2),
                                 pool_w[g, :, :].rearrange("(a p) c -> p a c", p=P)).then_inc(s_pw, 16)
                    for b in range(G_BLKS):
                        n = KV_BLKS + Q_BLKS + g * G_BLKS + b
                        load_block(h0 + n, b % RAW, w_in[n, :, :])

                def out_loads(nb, frames):
                    for k in range(KT):
                        kk = K_ORDER[k]
                        load_block(h0 + IN_BLKS + nb * KT + k, k % RAW,
                                   w_out[kk * P:(kk + 1) * P, bass.ds(nb * BLK, BLK)])
                        if k == X_LOAD and frames is not None:
                            sp.wait_ge(s_me, ONE + (h + 1) * 2 * GROUPS)
                            sp.wait_ge(s_xt, 1 + XG * (ROWT - 1 + nb))
                        if X_LOAD <= k < X_LOAD + OB and frames is not None:
                            cols = slice((k - X_LOAD) * BLK, (k - X_LOAD + 1) * BLK)
                            sp.dma_start(x_t[frames][:, cols],
                                         xcat[bass.ds(HALF + META + P * nb, P), cols]).then_inc(s_x[frames], 16)
                        if k == RES_LOAD:
                            sp.wait_ge(s_me, ONE + (h + 1) * 2 * GROUPS)
                            sp.wait_ge(s_free, ONE + (h * OB + nb) * ROWT)
                        if RES_LOAD <= k < RES_LOAD + ROWT:
                            r = k - RES_LOAD
                            sp.dma_start(y[r], xcat[h * HALF + META + P * r:h * HALF + META + P * (r + 1),
                                                    bass.ds(nb * BLK, BLK)]).then_inc(s_res[r], 16)

                if h == 0:
                    with sp.Fori(0, 2) as i:
                        for v in range(2):
                            nb = i * 2 + v
                            out_loads(nb, v)
                else:
                    with sp.Fori(0, OB) as nb:
                        out_loads(nb, None)

            for r in range(ROWT):
                sp.wait_ge(s_ye, YB_FREE + (HALVES * OB - 1) * ROWT + r + 1)
                sp.dma_start(out[SEQ - HALF + P * r:SEQ - HALF + P * (r + 1), (OB - 1) * BLK:],
                             y[r]).then_inc(s_last, 16)
            sp.wait_ge(s_last, 16 * ROWT)

        @block.gpsimd
        def _(pool):
            for first in from_one:
                pool.sem_inc(first, ONE)
            pool.sem_inc(s_qn, QB_FREE)
            pool.sem_inc(s_ye, YB_FREE)
            pool.memset(kT[:, :], 0.0).then_inc(s_init, 1)
            pool.memset(vT[:, :], 0.0).then_inc(s_init, 1)
            pool.memset(vm[:, :, :].bitcast(f32), 0.0).then_inc(s_init, 1)
            pool.memset(pm[:, :].bitcast(f32), 0.0).then_inc(s_init, 1)
            pool.memset(pnm[:, :, :], 0.0).then_inc(s_init, 1)
            chained = 0
            for h in range(HALVES):
                for g in range(GROUPS):
                    for jj in range(2):
                        pool.wait_ge(s_pve, ONE + (h * GROUPS + g) * 2 + jj + 1)
                        pool.wait_ge(s_d, ONE + (h * GROUPS + g) * 2 + jj)
                        src = pv[jj]
                        for lev in range(g + 1):
                            dst = psum_w[(g - lev) % 2]
                            step, lo = 2 ** lev, 2 ** (lev + 1) - 1
                            if lev:
                                pool.wait_ge(s_add, chained)
                            ins = pool.tensor_tensor(dst[:, lo:COLS], src[:, lo:COLS],
                                                     src[:, lo - step:COLS - step], ALU.add)
                            if lev < g:
                                ins.then_inc(s_add, 1)
                                chained += 1
                            else:
                                ins.then_inc(s_sum, 1)
                            src = dst
                if h == 0:
                    pool.wait_ge(s_me, ONE + 2 * GROUPS)
                    pool.dma_start(g_row, norm_g.partition_broadcast(P)).then_inc(s_g, 16)
                with pool.Fori(0, OB - h) as nb:
                    for r in range(ROWT):
                        pool.wait_ge(s_ye, YB_FREE + (h * OB + nb) * ROWT + r + 1)
                        pool.dma_start(out[h * HALF + P * r:h * HALF + P * (r + 1), bass.ds(nb * BLK, BLK)],
                                       y[r]).then_inc(s_out[r], 16)
                    for r in range(ROWT):
                        pool.wait_ge(s_out[r], 16 * (h * OB + nb + 1))
                        pool.sem_inc(s_free, 1)
            for r in range(ROWT):
                pool.wait_ge(s_out[r], 16 * (HALVES * OB - 1))

        @block.scalar
        def _(act):
            def copy(dst, src):
                return nc.scalar.activation(dst, src, ACT.Copy)

            def split_high(n4, off):
                slot = off % RAW
                act.wait_ge(s_raw[slot], 16 * (n4 + off // RAW + 1))
                if not (isinstance(n4, int) and n4 == 0 and off < SPLIT):
                    act.wait_ge(s_blk, ONE + n4 * RAW + (off - SPLIT + 1))
                copy(wh[:, slot, :], raw[:, slot, :]).then_inc(s_wh, 1)

            def stats(x, rows, squares, n, col, loaded, loads):
                act.wait_ge(loaded, 16 * loads)
                nc.scalar.activation(junk[0:rows, :], x[0:rows, :], ACT.Square,
                                     accum_out=xss[0:rows, col:col + 1]).then_inc(s_xsq, 1)
                act.wait_ge(s_xsq, squares + 1)
                if squares == 0:
                    act.wait_ge(s_cst, 32)
                root(rows, col)

            def root(rows, col):
                nc.scalar.activation(xsd[0:rows, col:col + 1], xss[0:rows, col:col + 1], ACT.Sqrt,
                                     scale=1.0 / D, bias=eps[0:rows, :]).then_inc(s_xsd, 1)

            def x_high(r, q, n):
                act.wait_ge(s_xt, n + 1)
                copy(act_h[:, 4 * q:4 * q + 4, bass.ds(META + P * r, P)],
                     XB[q].rearrange("p (k c) -> p k c", c=P)).then_inc(s_xh, 1)

            eps = cst[:, C_EPS:C_EPS + 1]
            act.wait_ge(s_init, 1)
            nc.scalar.activation(junk[:, 0:1], kT[:, 0:1], ACT.Sqrt).then_inc(s_table, 1)
            act.wait_ge(s_table, 1)

            for r in range(ROWT):
                if r == ROWT - 1:
                    act.wait_ge(s_xg, 1)
                    copy(act_h[:, :, 0:META], meta_g).then_inc(s_xh, 1)
                stats(x_first[r], P, r, r, r, s_xf[r], 1)
                if r == 0:
                    act.wait_ge(s_xm, 1)
                    root(META, ROWT)
            act.wait_ge(s_init, 5)
            for n in range(RAW):
                split_high(0, n)
            for k in range(KT):
                act.wait_ge(s_xt, k + 2)
                nc.scalar.activation(act_h[:, k, META:COLS], FB[k % 4], ACT.Copy,
                                     scale=vec[:, V_G + k:V_G + k + 1]).then_inc(s_xh, 1)
                if k in FIRST_SPLITS and FIRST_SPLITS[k] >= RAW:
                    split_high(0, FIRST_SPLITS[k])

            for h in range(HALVES):
                h4 = h * NBLK // RAW
                if h:
                    copy(kT[:, 0:CHUNK], kT[:, HALF:HALF + CHUNK]).then_inc(s_kd, 1)
                    copy(vT[:, 0:CHUNK], vT[:, HALF:HALF + CHUNK])
                act.wait_ge(s_mix, ONE + h * GROUPS * 2)
                copy(ones_r, cst[:, C_BLK:C_BLK + P]).then_inc(s_ones, 1)
                for s in range(4 if h == 0 else 0, 5):
                    split_high(h4, s + LEAD)
                product_done(act, h, 0)
                for bank, c in span_banks(h, KB[h]):
                    for dst in (k_sq, k_sqh):
                        nc.scalar.activation(dst[:, c], bank, ACT.Square).then_inc(s_ksq, 1)
                split_high(h4, 5 + LEAD)
                act.wait_ge(s_kss, h + 1)
                for bank, c in span_banks(h, (PT, PM)):
                    nc.scalar.activation(k_rs[:, c], bank, ACT.Sqrt,
                                         scale=1.0 / HD, bias=eps).then_inc(s_ksd, 1)
                for s in range(6, KV_BLKS):
                    split_high(h4, s + LEAD)
                product_done(act, h, TILE_BLKS)
                for bank, c in span_banks(h, VB[h]):
                    own_v, frames = own_part(bank, c)
                    copy(vT[:, CHUNK + frames.start:CHUNK + frames.stop], own_v).then_inc(s_vT, 1)
                if h == 0:
                    copy(v_meta[:, :], R[2][:, 0:META]).then_inc(s_vT, 1)

                def v_all_out():
                    act.wait_ge(s_vt, h + 1)
                    act.wait_ge(s_free, ONE + h * OB * ROWT)
                    copy(vm_all, R[2][0:META, 0:P]).then_inc(s_va, 1)
                    copy(v_all, S[:, :, :].rearrange("p b (c n) -> p (b c) n", c=4)).then_inc(s_va, 1)

                def k_band():
                    act.wait_ge(s_kn, SPANS_BY[h + 1])
                    for e in range(KVH):
                        src = slice(e * HD, (e + 1) * HD)
                        for band, dst in ((band_h, slice(0, HD)), (band_x, slice(HD, P))):
                            kb = band[dst, e, :].rearrange("p (c n) -> p c n", n=BAND)
                            copy(kb[:, :, 0:CHUNK],
                                 kT[src, :].rearrange("p (c n) -> p c n", n=CHUNK)).then_inc(s_kbh, 1)
                            copy(kb[:, :, CHUNK:BAND],
                                 k_meta[src, :].unsqueeze(1).to_broadcast([HD, NCH + 1, META])).then_inc(s_kbh, 1)

                def v_operand(e):
                    act.wait_ge(s_o, ONE + (h * KVH + e) * 2 * UNITS)
                    copy(v_s[:, :, 0, :], v_all[:, :, e * HD:(e + 1) * HD]).then_inc(s_vh, 1)
                    for at in (0, 32):
                        copy(vm[at:at + META, 0, :], vm_all[:, e * HD:(e + 1) * HD]).then_inc(s_vh, 1)

                def q_square(t):
                    product_done(act, h, KV_BLKS + t * TILE_BLKS)
                    if t >= 2:
                        act.wait_ge(s_qss, h * PAIRS + t - 1)
                    for dst in (q_sq[t % 2], q_sqh[t % 2]):
                        nc.scalar.activation(dst, QB[t % 4][:, :], ACT.Square).then_inc(s_qsq, 1)

                def q_sqrt(t):
                    act.wait_ge(s_qss, h * PAIRS + t + 1)
                    act.wait_ge(s_qn, QB_FREE + h * PAIRS + max(t - 1, 0))
                    nc.scalar.activation(q_rs[t % 2], (PT, PM)[t % 2][:, :], ACT.Sqrt,
                                         scale=1.0 / HD, bias=eps).then_inc(s_qsd, 1)

                for s in range(Q_BLKS + 1):
                    if s and s % 4 == 0:
                        q_square(s // 4 - 1)
                    if s < Q_BLKS:
                        split_high(h4 + KV_BLKS // RAW, s + LEAD)
                    if s > 4 and s % 4 == 1:
                        q_sqrt(s // 4 - 1)
                    if s == 2:
                        v_all_out()
                    if s == 18:
                        k_band()
                    if s == 23:
                        v_operand(0)
                q_sqrt(PAIRS - 1)
                act.wait_ge(s_qn, QB_FREE + (h + 1) * PAIRS - 1)

                def mix_high(m):
                    k = m % KT if isinstance(m, int) else m[1]
                    m = m if isinstance(m, int) else m[0] * KT + m[1]
                    if isinstance(m, int) and m < 4:
                        if m < 2:
                            act.wait_ge(s_s, ONE + (h + 1) * GROUPS * UNITS)
                        else:
                            act.wait_ge(s_o, ONE + (h + 1) * GROUPS * UNITS)
                    else:
                        act.wait_ge(s_blk, ONE + h * NBLK + IN_BLKS + m - 3)
                    if k == 12:
                        act.wait_ge(s_me, ONE + (h + 1) * GROUPS * 2)
                    if k == 14:
                        act.wait_ge(s_oe, ONE + (h + 1) * GROUPS * UNITS)
                    copy(mix_h[k % 4], mixed[:, K_ORDER[k], :]).then_inc(s_mh, 1)

                def group(g):
                    G = h * GROUPS + g
                    n0 = KV_BLKS + Q_BLKS + g * G_BLKS
                    n4 = h4 + (KV_BLKS + Q_BLKS) // RAW + g * (G_BLKS // RAW)

                    def q_unit(u):
                        act.wait_ge(s_s, ONE + G * UNITS + u)
                        q = mixed[:, bass.ds(PAIRS + g * 2 + u // 2, 1),
                                  (u % 2) * 256:(u % 2) * 256 + 256].rearrange(
                                      "p a (c t) -> p (a c) t", t=CHUNK)
                        copy(qs[0:HD, :, 0, :], q[0:HD]).then_inc(s_quh, 1)
                        copy(qs[0:HD, :, 1, :], q[HD:P]).then_inc(s_quh, 1)
                        copy(qs[HD:P, :, 1, :], q[HD:P]).then_inc(s_quh, 1)

                    def exps(u):
                        act.wait_ge(s_nm, G * UNITS + u + 1)
                        sink = vec[:, bass.ds(V_SINK + g * 2 + u // 2, 1)]
                        for c in range(QUAD):
                            nc.scalar.activation(
                                prob[:, c, :], S[:, c // 2, (c % 2) * KEYS:(c % 2 + 1) * KEYS], ACT.Exp,
                                bias=nmax[:, c:c + 1], accum_out=den[:, c:c + 1]).then_inc(s_ex, 1)
                        nc.scalar.activation(esink[:, :], nmax[:, :], ACT.Exp, bias=sink).then_inc(s_ex, 1)

                    def p_high(u):
                        act.wait_ge(s_tp, ONE + G * UNITS + u + 1)
                        act.wait_ge(s_o, ONE + G * UNITS + u)
                        copy(pt[:, :, 0, :], PT[:, :].rearrange("p (c n) -> p c n", c=QUAD)).then_inc(s_ph, 1)
                        for at in (0, 64):
                            for c in range(QUAD):
                                copy(pm[at:at + META, c * P:(c + 1) * P],
                                     PM[32 * c:32 * c + META, 0:P]).then_inc(s_ph, 1)

                    def o_low(u):
                        act.wait_ge(s_o, ONE + G * UNITS + u + 1)
                        act.wait_ge(s_oe, ONE + G * UNITS + u)
                        copy(o_part[:, :].rearrange("p (c n) -> p c n", c=QUAD), OV[HD:P, :, 0, :]).then_inc(s_ol, 1)

                    def gate_exp(n, bank):
                        product_done(act, h, n0 + (0, 4, 16, 20)[n])
                        if n < 2:
                            act.wait_ge(s_oe, ONE + G * UNITS)
                        else:
                            act.wait_ge(s_me, ONE + G * 2)
                        nc.scalar.activation(gate[n], bank[:, :], ACT.Exp, scale=-1.0).then_inc(s_ge[n], 1)

                    def pv_out(jj):
                        product_done(act, h, n0 + 8 + 4 * jj)
                        act.wait_ge(s_dl, ONE + G * 2)
                        for bank, c in span_banks(h, PVB[h][jj]):
                            copy(pv[jj][:, c], bank)
                        last = pv_last[:, bass.ds(g * 2 + jj, 1), :]
                        if h == 0:
                            ins = copy(last, bank[:, SUB - META:SUB].unsqueeze(1))
                        else:
                            ins = copy(pv[jj][:, 0:META].unsqueeze(1), last)
                        ins.then_inc(s_pve, 1)

                    def d_high(jj):
                        act.wait_ge(s_d, ONE + G * 2 + jj + 1)
                        act.wait_ge(s_mix, ONE + G * 2)
                        copy(d_h[:, jj, :], pv[jj][:, META:COLS]).then_inc(s_dh, 1)

                    def pw_high():
                        act.wait_ge(s_pw, 16 * (G + 1))
                        act.wait_ge(s_mix, ONE + G * 2)
                        copy(pw_h[:, :], pw_raw).then_inc(s_pwh, 1)

                    todo = {s: [] for s in range(G_BLKS + 1)}
                    for u in range(UNITS):
                        todo[4 * u + 1].append((q_unit, u))
                        todo[4 * u + 5].append((exps, u))
                        todo[4 * u + 9].append((p_high, u))
                        todo[4 * u + 11].append((o_low, u))
                    todo[2].append((pw_high,))
                    todo[4].append((gate_exp, 0, R[0]))
                    todo[8].append((gate_exp, 1, R[1]))
                    todo[16].append((d_high, 0))
                    todo[20].append((gate_exp, 2, R[0]))
                    todo[20].append((d_high, 1))
                    todo[24].append((gate_exp, 3, R[1]))
                    if isinstance(g, int) and g == 2:
                        todo[2].append((v_operand, 1))
                    if isinstance(g, int) and g == 3:
                        for m, s in enumerate((21, 22, 24)):
                            todo[s].insert(0, (mix_high, m))
                    for s in range(G_BLKS + 1):
                        if s == 12:
                            pv_out(0)
                        elif s == 16:
                            pv_out(1)
                        if s < G_BLKS:
                            split_high(n4, s + LEAD)
                        for f, *a in todo[s]:
                            f(*a)

                with act.Fori(0, 2) as g:
                    group(g)
                act.wait_ge(s_qn, QB_FREE + (h + 1) * PAIRS)
                group(2)
                group(3)

                def out_splits(nb, frames, last, turn=0):
                    for k in range(KT):
                        if h == 0 or not last or k < KT - LEAD:
                            split_high(h4 + IN_BLKS // RAW + nb * (KT // RAW), k + LEAD)
                        if k + LEAD < KT:
                            mix_high(nb * KT + k + LEAD if isinstance(nb, int) else (nb, k + LEAD))
                        elif not last:
                            mix_high((nb + 1, k + LEAD - KT))
                        if frames is not None:
                            if k == X_AT[frames] - 4:
                                stats(x_t[frames], P, ROWT + nb, ROWT + 1 + nb, frames, s_x[frames],
                                      OB * (1 + turn))
                            q = k - X_AT[frames] - 2
                            if 0 <= q < XG:
                                x_high(nb, q, 1 + XG * (ROWT + nb) + q)

                if h == 0:
                    for nb in range(OB):
                        out_splits(nb, nb % 2, nb == OB - 1, nb // 2)
                else:
                    with act.Fori(0, OB - 1) as nb:
                        out_splits(nb, None, False)
                    out_splits(OB - 1, None, True)

        @block.vector
        def _(dve):
            def sub(dst, a, b):
                return nc.vector.tensor_tensor(dst, a, b, ALU.subtract)

            def split_low(n4, off):
                slot = off % RAW
                dve.wait_ge(s_wh, n4 * RAW + off + 1)
                sub(wl[:, slot, :], raw[:, slot, :], wh[:, slot, :]).then_inc(s_wl, 1)

            def norm(slot, rows, n):
                dve.wait_ge(s_xsd, n + 1)
                nc.vector.reciprocal(xrs[0:rows, slot:slot + 1], xsd[0:rows, slot:slot + 1]).then_inc(s_xrs, 1)
                dve.wait_ge(s_xrs, n + 1)
                dve.wait_ge(s_g, 16)
                nc.vector.scalar_tensor_tensor(x_t[slot][0:rows, :], x_t[slot][0:rows, :],
                                               xrs[0:rows, slot:slot + 1], g_row[0:rows, :],
                                               ALU.mult, ALU.mult).then_inc(s_xn, 1)

            def x_low(r, q, n):
                dve.wait_ge(s_xh, n + 1)
                cols = bass.ds(META + P * r, P)
                sub(act_l[:, 4 * q:4 * q + 4, cols], XB[q].rearrange("p (k c) -> p k c", c=P),
                    act_h[:, 4 * q:4 * q + 4, cols]).then_inc(s_xl, 1)

            dve.wait_ge(s_xf[ROWT], 16)
            nc.vector.tensor_tensor(meta_sq, x_meta, x_meta, ALU.mult).then_inc(s_xmm, 1)
            dve.wait_ge(s_xmm, 1)
            nc.vector.tensor_reduce(xss[0:META, ROWT:ROWT + 1], meta_sq, AX.X, ALU.add).then_inc(s_xm, 1)

            dve.wait_ge(s_cst, 32)
            dve.wait_ge(s_init, 5)
            nc.vector.tensor_scalar(gq8[:, :], vec[:, V_GQ:V_GQ + 1], HD ** -0.5, None, ALU.mult).then_inc(s_gq, 1)
            dve.wait_ge(s_gq, 1)

            def first_norm(x, rows, n, col):
                dve.wait_ge(s_xsd, n + 1)
                nc.vector.reciprocal(xrs[0:rows, col:col + 1], xsd[0:rows, col:col + 1]).then_inc(s_xrs, 1)
                dve.wait_ge(s_xrs, n + 1)
                nc.vector.tensor_scalar(x[0:rows, :], x[0:rows, :], xrs[0:rows, col:col + 1], None,
                                        ALU.mult).then_inc(s_xn, 1)

            first_norm(x_first[0], P, 0, 0)
            first_norm(x_meta, META, 1, ROWT)
            first_norm(x_first[1], P, 2, 1)
            dve.wait_ge(s_xt, 1)
            nc.vector.tensor_tensor(meta_g, R[2][:, 0:KT * META].rearrange("p (k c) -> p k c", c=META),
                                    vec[:, V_G:V_G + KT].unsqueeze(2).to_broadcast([P, KT, META]),
                                    ALU.mult).then_inc(s_xg, 1)
            first_norm(x_first[2], P, 3, 2)
            dve.wait_ge(s_xh, 1)
            sub(act_l[:, :, 0:META], meta_g, act_h[:, :, 0:META]).then_inc(s_xl, 1)
            first_norm(x_first[3], P, 4, 3)
            for n in range(2):
                split_low(0, n)
            for k in range(KT):
                dve.wait_ge(s_xh, k + 2)
                nc.vector.scalar_tensor_tensor(act_l[:, k, META:COLS], FB[k % 4], vec[:, V_G + k:V_G + k + 1],
                                               act_h[:, k, META:COLS], ALU.mult, ALU.subtract).then_inc(s_xl, 1)
                if k in FIRST_SPLITS:
                    split_low(0, FIRST_SPLITS[k])

            for h in range(HALVES):
                h4 = h * NBLK // RAW
                gk = vec[:, V_GK:V_GK + 1]
                for s in range(4 if h == 0 else 0, 5):
                    split_low(h4, s + LEAD)
                for n, c in enumerate(SPANS[h]):
                    dve.wait_ge(s_ksq, 2 * (SPANS_BY[h] + n + 1))
                    sub(k_sql[:, c], k_sq[:, c], k_sqh[:, c]).then_inc(s_ksl, 1)
                for s in range(5, 7):
                    split_low(h4, s + LEAD)
                if h:
                    dve.wait_ge(s_kd, 1)
                for n, (bank, c) in enumerate(span_banks(h, KB[h])):
                    dve.wait_ge(s_ksd, SPANS_BY[h] + n + 1)
                    nc.vector.reciprocal(k_rs[:, c], k_rs[:, c]).then_inc(s_krs, 1)
                    dve.wait_ge(s_krs, SPANS_BY[h] + n + 1)
                    if c.start == 0:
                        nc.vector.scalar_tensor_tensor(k_meta[:, :], bank[:, 0:META], gk,
                                                       k_rs[:, 0:META], ALU.mult, ALU.mult)
                    own_k, frames = own_part(bank, c)
                    nc.vector.scalar_tensor_tensor(kT[:, CHUNK + frames.start:CHUNK + frames.stop], own_k, gk,
                                                   k_rs[:, META + frames.start:META + frames.stop],
                                                   ALU.mult, ALU.mult).then_inc(s_kn, 1)
                split_low(h4, 7 + LEAD)

                def k_band():
                    for e in range(KVH):
                        src = slice(e * HD, (e + 1) * HD)
                        high = (band_h, band_x)[e][src, e, :].rearrange("p (c n) -> p c n", n=BAND)
                        low = band_x[0:HD, e, :].rearrange("p (c n) -> p c n", n=BAND)
                        dve.wait_ge(s_kbh, 8 * h + (2, 8)[e])
                        sub(low[:, :, 0:CHUNK], kT[src, :].rearrange("p (c n) -> p c n", n=CHUNK),
                            high[:, :, 0:CHUNK])
                        ins = sub(low[:, :, CHUNK:BAND],
                                  k_meta[src, :].unsqueeze(1).to_broadcast([HD, NCH + 1, META]),
                                  high[:, :, CHUNK:BAND])
                    ins.then_inc(s_kbl, 1)

                def v_operand(e):
                    dve.wait_ge(s_vh, 3 * (h * KVH + e + 1))
                    sub(v_s[:, :, 1, :], v_all[:, :, e * HD:(e + 1) * HD], v_s[:, :, 0, :])
                    sub(vm[64:64 + META, 0, :], vm_all[:, e * HD:(e + 1) * HD], vm[0:META, 0, :]).then_inc(s_vl, 1)

                def square_low(t):
                    dve.wait_ge(s_qsq, 2 * (h * PAIRS + t + 1))
                    sub(q_sql[t % 2], q_sq[t % 2], q_sqh[t % 2]).then_inc(s_qsl, 1)

                def q_norm(t):
                    n = h * PAIRS + t
                    dve.wait_ge(s_qsd, n + 1)
                    nc.vector.reciprocal(q_rs[t % 2], q_rs[t % 2]).then_inc(s_qrs, 1)
                    dve.wait_ge(s_qrs, n + 1)
                    nc.vector.scalar_tensor_tensor(mixed[:, PAIRS + t, :], QB[t % 4][:, :], gq8[:, :],
                                                   q_rs[t % 2], ALU.mult, ALU.mult).then_inc(s_qn, 1)

                for s in range(Q_BLKS + 1):
                    if s and s % 4 == 0:
                        square_low(s // 4 - 1)
                    if s < Q_BLKS:
                        split_low(h4 + KV_BLKS // RAW, s + LEAD)
                    if s > 4 and s % 4 == 2:
                        q_norm(s // 4 - 1)
                    if s == 21:
                        k_band()
                    if s == 25:
                        v_operand(0)
                q_norm(PAIRS - 1)

                def mix_low(m):
                    k = m % KT if isinstance(m, int) else m[1]
                    m = m if isinstance(m, int) else m[0] * KT + m[1]
                    dve.wait_ge(s_mh, h * OB * KT + m + 1)
                    sub(mix_l[k % 4], mixed[:, K_ORDER[k], :], mix_h[k % 4]).then_inc(s_ml, 1)

                def mix_out(g, jj, bank):
                    G = h * GROUPS + g
                    dve.wait_ge(s_mix, ONE + G * 2 + jj + 1)
                    dve.wait_ge(s_gt[2 + jj], ONE + G + 1)
                    nc.vector.scalar_tensor_tensor(
                        mixed[:, bass.ds(g * 2 + jj, 1), :], bank[:, :].unsqueeze(1),
                        vec[:, bass.ds(V_SCALE + g * 2 + jj, 1)], gate[2 + jj].unsqueeze(1),
                        ALU.mult, ALU.mult).then_inc(s_me, 1)

                def group(g):
                    G = h * GROUPS + g
                    n4 = h4 + (KV_BLKS + Q_BLKS) // RAW + g * (G_BLKS // RAW)

                    def q_unit(u):
                        dve.wait_ge(s_quh, (G * UNITS + u + 1) * 3)
                        q = mixed[:, bass.ds(PAIRS + g * 2 + u // 2, 1),
                                  (u % 2) * 256:(u % 2) * 256 + 256].rearrange(
                                      "p a (c t) -> p (a c) t", t=CHUNK)
                        sub(qs[HD:P, :, 0, :], q[0:HD], qs[0:HD, :, 0, :])
                        sub(qs[HD:P, :, 1, :], q[HD:P], qs[HD:P, :, 1, :]).then_inc(s_qul, 1)

                    def row_max(u):
                        dve.wait_ge(s_s, ONE + G * UNITS + u + 1)
                        nc.vector.tensor_reduce(
                            smax[:, :].rearrange("p (b c) -> p b c", b=2),
                            S[:, :, 0:2 * KEYS].rearrange("p b (c k) -> p b c k", c=2),
                            AX.X, ALU.max).then_inc(s_mx, 1)
                        dve.wait_ge(s_mx, G * UNITS + u + 1)
                        sink = vec[:, bass.ds(V_SINK + g * 2 + u // 2, 1)]
                        nc.vector.tensor_scalar(nmax[:, :], smax[:, :], sink, -1.0,
                                                ALU.max, ALU.mult).then_inc(s_nm, 1)

                    def normalise(u):
                        n = G * UNITS + u
                        dve.wait_ge(s_ex, ONE + (n + 1) * (QUAD + 1))
                        nc.vector.tensor_tensor(dtot[:, :], den[:, :], esink[:, :], ALU.add).then_inc(s_dt, 1)
                        dve.wait_ge(s_dt, n + 1)
                        nc.vector.reciprocal(rden[:, :], dtot[:, :]).then_inc(s_rd, 1)
                        dve.wait_ge(s_rd, n + 1)
                        dve.wait_ge(s_tp, ONE + n)
                        r = rden[:, :].unsqueeze(2)
                        pc = pn.rearrange("p (c k) -> p c k", c=QUAD)
                        nc.vector.tensor_tensor(pc[:, :, 0:CHUNK], prob[:, :, 0:CHUNK],
                                                r.to_broadcast([P, QUAD, CHUNK]), ALU.mult)
                        nc.vector.tensor_tensor(pc[:, :, CHUNK:P], prob[:, :, BAND:KEYS],
                                                r.to_broadcast([P, QUAD, CHUNK]), ALU.mult)
                        nc.vector.tensor_tensor(pnm[:, :, 0:META],
                                                prob[:, :, CHUNK:BAND],
                                                r.to_broadcast([P, QUAD, META]), ALU.mult).then_inc(s_pn, 1)

                    def p_low(u):
                        dve.wait_ge(s_ph, (G * UNITS + u + 1) * (1 + 2 * QUAD))
                        sub(pt[:, :, 1, :], PT[:, :].rearrange("p (c n) -> p c n", c=QUAD), pt[:, :, 0, :])
                        for c in range(QUAD):
                            cs = slice(c * P, (c + 1) * P)
                            ins = sub(pm[32:32 + META, cs], PM[32 * c:32 * c + META, 0:P], pm[0:META, cs])
                        ins.then_inc(s_pl, 1)

                    def o_out(u):
                        dve.wait_ge(s_o, ONE + G * UNITS + u + 1)
                        dve.wait_ge(s_gt[u // 2], ONE + G + 1)
                        cols = slice((u % 2) * 256, (u % 2) * 256 + 256)
                        dve.wait_ge(s_ol, G * UNITS + u + 1)
                        o = o_part[:, :].rearrange("p (c n) -> p c n", c=QUAD)
                        nc.vector.tensor_tensor(o, OV[0:HD, :, 1, :], o, ALU.add).then_inc(s_oa, 1)
                        dve.wait_ge(s_oa, 3 * (G * UNITS + u) + 1)
                        for head in range(2):
                            part, cut = slice(head * HD, (head + 1) * HD), slice(head * CHUNK, (head + 1) * CHUNK)
                            nc.vector.tensor_tensor(
                                o_sum[part].rearrange("p (c t) -> p c t", t=CHUNK),
                                OV[0:HD, :, 0, cut], o[:, :, cut], ALU.add).then_inc(s_oa, 1)
                        dve.wait_ge(s_oa, 3 * (G * UNITS + u + 1))
                        nc.vector.tensor_tensor(mixed[:, bass.ds(PAIRS + g * 2 + u // 2, 1), cols],
                                                o_sum.unsqueeze(1), gate[u // 2][:, cols].unsqueeze(1),
                                                ALU.mult).then_inc(s_oe, 1)

                    def silu(n, bank):
                        dve.wait_ge(s_ge[n], G + 1)
                        nc.vector.tensor_scalar(gate[n], gate[n], 1.0, None, ALU.add).then_inc(s_ga, 1)
                        dve.wait_ge(s_ga, G * 4 + n + 1)
                        nc.vector.reciprocal(gate[n], gate[n]).then_inc(s_gr, 1)
                        dve.wait_ge(s_gr, G * 4 + n + 1)
                        nc.vector.tensor_tensor(gate[n], bank[:, :], gate[n], ALU.mult).then_inc(s_gt[n], 1)

                    def pooled(jj):
                        dve.wait_ge(s_sum, G * 2 + jj + 1)
                        nc.vector.scalar_tensor_tensor(
                            pv[jj][:, META:COLS], psum_w[0][:, META:COLS],
                            cst[:, bass.ds(C_INVW + g, 1)], pv[jj][:, META:COLS],
                            ALU.mult, ALU.subtract).then_inc(s_d, 1)

                    def d_low(jj):
                        dve.wait_ge(s_dh, G * 2 + jj + 1)
                        sub(d_l[:, jj, :], pv[jj][:, META:COLS], d_h[:, jj, :]).then_inc(s_dl, 1)

                    def pw_low():
                        dve.wait_ge(s_pwh, G + 1)
                        sub(pw_l[:, :], pw_raw, pw_h[:, :]).then_inc(s_pwl, 1)

                    todo = {s: [] for s in range(G_BLKS + 1)}
                    for u in range(UNITS):
                        todo[4 * u + 1].append((q_unit, u))
                        todo[4 * u + 4].append((row_max, u))
                        todo[4 * u + 6].append((normalise, u))
                        todo[4 * u + 9].append((p_low, u))
                        todo[4 * u + 11].append((o_out, u))
                    todo[2].append((pw_low,))
                    todo[4].append((silu, 0, R[0]))
                    todo[8].append((silu, 1, R[1]))
                    todo[15].append((pooled, 0))
                    todo[17].append((d_low, 0))
                    todo[19].append((pooled, 1))
                    todo[21].append((d_low, 1))
                    todo[21].append((silu, 2, R[0]))
                    todo[24].append((silu, 3, R[1]))
                    if isinstance(g, int) and g == 2:
                        todo[4].append((v_operand, 1))
                    if isinstance(g, int) and g == 3:
                        for m, s in enumerate((21, 22, 24)):
                            todo[s].insert(0, (mix_low, m))
                    else:
                        todo[24] += [(mix_out, g, 0, PT), (mix_out, g, 1, R[2])]
                    for s in range(G_BLKS + 1):
                        if s < G_BLKS:
                            split_low(n4, s + LEAD)
                        for f, *a in todo[s]:
                            f(*a)

                with dve.Fori(0, 2) as g:
                    group(g)
                group(2)
                group(3)

                def add_residual(nb, r):
                    if r < ROWT - 1:
                        dve.wait_ge(s_y, (h * OB + nb) * (ROWT - 1) + r + 1)
                    else:
                        dve.wait_ge(s_blk, ONE + h * NBLK + IN_BLKS + (nb + 1) * KT)
                    dve.wait_ge(s_res[r], 16 * (h * OB + nb + 1))
                    nc.vector.tensor_tensor(y[r], YB[r], y[r], ALU.add).then_inc(s_ye, 1)

                def out_splits(nb, frames, last, turn=0):
                    for k in range(KT):
                        if k == KT - 1:
                            for r in range(ROWT):
                                add_residual(nb, r)
                        if h == 0 or not last or k < KT - LEAD:
                            split_low(h4 + IN_BLKS // RAW + nb * (KT // RAW), k + LEAD)
                        if k + LEAD < KT:
                            mix_low(nb * KT + k + LEAD if isinstance(nb, int) else (nb, k + LEAD))
                        elif not last:
                            mix_low((nb + 1, k + LEAD - KT))
                        if isinstance(nb, int) and nb == 0 and k == 0:
                            mix_out(GROUPS - 1, 0, PT)
                            mix_out(GROUPS - 1, 1, R[2])
                        if frames is not None:
                            if k == X_AT[frames] - 2:
                                norm(frames, P, ROWT + 1 + nb)
                            q = k - X_AT[frames] - 2
                            if 0 <= q < XG:
                                x_low(nb, q, 1 + XG * (ROWT + nb) + q)

                if h == 0:
                    for nb in range(OB):
                        out_splits(nb, nb % 2, nb == OB - 1, nb // 2)
                else:
                    out_splits(0, None, False)
                    with dve.Fori(1, OB - 1) as nb:
                        out_splits(nb, None, False)
                    out_splits(OB - 1, None, True)

        @block.tensor
        def _(pe):
            mm = nc.tensor.matmul

            def tile(h, n, banks, cols, events=None, slot0=0, before=None, after=None):
                for b in range(TILE_BLKS):
                    pe.wait_ge(s_wl, ONE + h * NBLK + n + b + 1)
                    for kk in range(4):
                        k = 4 * b + kk
                        w = slice(kk * P, (kk + 1) * P)
                        if before:
                            before(k)
                        for bank, c in zip(banks, cols):
                            o = bank[:, 0:c.stop - c.start]
                            mm(o, wh[:, b, w], act_h[:, k, c], start=(k == 0), stop=False)
                            mm(o, wh[:, b, w], act_l[:, k, c], start=False, stop=False)
                        for bank, c in zip(banks, cols):
                            o = bank[:, 0:c.stop - c.start]
                            last = mm(o, wl[:, b, w], act_h[:, k, c], start=False, stop=(k == KT - 1))
                        if kk == 3:
                            last.then_inc(s_blk, 1)
                        if after:
                            after(k)
                    if events:
                        events(slot0 + b)

            own = (slice(META, COLS),)

            def x_group(slot, q):
                for kk in range(4):
                    k = 4 * q + kk
                    last = nc.tensor.transpose(XB[q][:, kk * P:(kk + 1) * P],
                                               x_t[slot][:, k * P:(k + 1) * P], ident)
                last.then_inc(s_xt, 1)

            pe.wait_ge(s_cst, 32)
            pe.wait_ge(s_init, 5)

            pe.wait_ge(s_xn, 2)
            for k in range(KT):
                last = nc.tensor.transpose(R[2][:, k * META:(k + 1) * META],
                                           x_meta[:, k * P:(k + 1) * P], ident[0:META, 0:META])
            last.then_inc(s_xt, 1)

            def first_group(k):
                for r in range(ROWT):
                    last = nc.tensor.transpose(FB[k % 4][:, r * P:(r + 1) * P],
                                               x_first[r][:, k * P:(k + 1) * P], ident)
                last.then_inc(s_xt, 1)

            pe.wait_ge(s_xn, ROWT + 1)
            for k in range(4):
                first_group(k)

            def split_done(k):
                pe.wait_ge(s_xl, k + 2)

            def next_group(k):
                if k + 4 < KT:
                    first_group(k + 4)

            for h in range(HALVES):
                if h:
                    pe.wait_ge(s_xl, 1 + XG * ROWT * 2)

                def k_squares(s):
                    if s == TILE_BLKS:
                        pe.wait_ge(s_ones, h + 1)
                        pe.wait_ge(s_ksl, SPANS_BY[h + 1])
                        for bank, c in span_banks(h, (PT, PM)):
                            mm(bank, ones_r, k_sqh[:, c], start=True, stop=False)
                            last = mm(bank, ones_r, k_sql[:, c], start=False, stop=True)
                        last.then_inc(s_kss, 1)

                if h == 0:
                    tile(h, 0, KB[h], SPANS[h], before=split_done, after=next_group)
                else:
                    tile(h, 0, KB[h], SPANS[h])
                tile(h, TILE_BLKS, VB[h], SPANS[h], events=k_squares, slot0=TILE_BLKS)
                if h:
                    pe.wait_ge(s_ye, YB_FREE + OB * ROWT)

                def v_windows():
                    pe.wait_ge(s_vT, V_OUT[h])
                    nc.tensor.transpose(R[2][0:META, 0:P], v_meta[:, :], ident)
                    for c in range(NCH):
                        last = nc.tensor.transpose(S[:, c // 4, (c % 4) * P:(c % 4 + 1) * P],
                                                   vT[:, c * CHUNK:c * CHUNK + P], ident)
                    last.then_inc(s_vt, 1)

                def sum_squares(t):
                    pe.wait_ge(s_qsl, h * PAIRS + t + 1)
                    if t == 0:
                        pe.wait_ge(s_ksd, SPANS_BY[h + 1])
                    if t >= 2:
                        pe.wait_ge(s_qsd, h * PAIRS + t - 1)
                    bank = (PT, PM)[t % 2][:, :]
                    mm(bank, ones_r, q_sqh[t % 2], start=True, stop=False)
                    mm(bank, ones_r, q_sql[t % 2], start=False, stop=True).then_inc(s_qss, 1)

                def q_events(s):
                    if s == 0:
                        v_windows()
                    elif s % 4 == 0:
                        sum_squares(s // 4 - 1)

                for t in range(PAIRS):
                    pe.wait_ge(s_qn, QB_FREE + h * PAIRS + t - 3)
                    if t == 0 and h == 0:
                        pe.wait_ge(s_kn, 1)
                    elif t == 1:
                        pe.wait_ge(s_vT, V_OUT[h])
                    elif t == 2:
                        pe.wait_ge(s_kn, SPANS_BY[h + 1])
                    elif t == 3:
                        pe.wait_ge(s_va, 2 * (h + 1))
                    tile(h, KV_BLKS + t * TILE_BLKS, (QB[t % 4],), own, events=q_events, slot0=4 * t)

                def group(g, e, late):
                    G = h * GROUPS + g

                    def scores(u):
                        pe.wait_ge(s_qul, G * UNITS + u + 1)
                        pe.wait_ge(s_ex, ONE + (G * UNITS + u) * (QUAD + 1))
                        pe.wait_ge(s_kbh, 8 * (h + 1))
                        pe.wait_ge(s_kbl, ONE + h + 1)
                        for c in range(QUAD):
                            ch = (u % 2) * QUAD + c
                            o = S[:, c // 2, (c % 2) * KEYS:(c % 2 + 1) * KEYS]
                            at = slice(ch * BAND, ch * BAND + KEYS)
                            q = qs[:, c, :, :].rearrange("p a t -> p (a t)")
                            masked = h == 0 and ch == 0
                            mm(o, q[0:HD], band_h[0:HD, e, at], start=True, stop=False)
                            last = mm(o, q, band_x[:, e, at], start=False, stop=not masked)
                            if masked:
                                last = mm(o, ident, cst[:, C_MASK:C_MASK + KEYS],
                                          start=False, stop=True)
                        last.then_inc(s_s, 1)

                    def transposes(u):
                        n = G * UNITS + u
                        pe.wait_ge(s_pn, n + 1)
                        pe.wait_ge(s_pl, ONE + n)
                        pe.wait_ge(s_oe, ONE + n)
                        pe.wait_ge(s_me, ONE + G * 2)
                        for c in range(QUAD):
                            nc.tensor.transpose(PT[:, c * P:(c + 1) * P], pn[:, c * P:(c + 1) * P], ident)
                        nc.tensor.transpose(PM[:, 0:P], pnm[:, :, :].rearrange("p c k -> p (c k)"),
                                            ident).then_inc(s_tp, 1)

                    def values(u):
                        n = G * UNITS + u
                        pe.wait_ge(s_pl, ONE + n + 1)
                        pe.wait_ge(s_vl, h * KVH + e + 1)
                        for c in range(QUAD):
                            ch = (u % 2) * QUAD + c
                            mm(OV[:, c, :, :].rearrange("p s n -> p (s n)"),
                               v_s[:, ch, :, :].rearrange("p a d -> p (a d)"),
                               pt[:, c, :, :].rearrange("p s n -> p (s n)"), start=(c % 2 == 0), stop=False)
                        for b in range(2):
                            last = mm(OV[:, 2 * b:2 * b + 2, 0, :], vm[:, :, :].rearrange("p a d -> p (a d)"),
                                      pm[:, 2 * b * P:2 * (b + 1) * P].rearrange("p (c n) -> p c n", c=2),
                                      start=False, stop=True)
                        last.then_inc(s_o, 1)

                    when = {}
                    for u in range(UNITS):
                        when.setdefault(4 * u + 3, []).append((scores, u))
                        when.setdefault(4 * u + 8, []).append((transposes, u))
                        when.setdefault(4 * u + 10, []).append((values, u))

                    if late:
                        when[0] = [(sum_squares, PAIRS - 1)]

                    def events(s):
                        for f, u in when.get(s, ()):
                            f(u)

                    n0 = KV_BLKS + Q_BLKS + g * G_BLKS
                    pe.wait_ge(s_qn, QB_FREE + h * PAIRS + 5)
                    pe.wait_ge(s_gt[2], ONE + G)
                    tile(h, n0, (R[0],), own, events=events, slot0=0)
                    pe.wait_ge(s_qn, QB_FREE + h * PAIRS + 7)
                    pe.wait_ge(s_gt[3], ONE + G)
                    tile(h, n0 + 4, (R[1],), own, events=events, slot0=4)
                    pe.wait_ge(s_qn, QB_FREE + h * PAIRS + 8)
                    pe.wait_ge(s_gt[0], ONE + G + 1)
                    pe.wait_ge(s_me, ONE + G * 2)
                    tile(h, n0 + 8, PVB[h][0], SPANS[h], events=events, slot0=8)
                    pe.wait_ge(s_gt[1], ONE + G + 1)
                    pe.wait_ge(s_pve, ONE + G * 2 + 1)
                    tile(h, n0 + 12, PVB[h][1], SPANS[h], events=events, slot0=12)
                    tile(h, n0 + 16, (R[0],), own, events=events, slot0=16)
                    pe.wait_ge(s_pve, ONE + G * 2 + 2)
                    tile(h, n0 + 20, (R[1],), own, events=events, slot0=20)
                    pe.wait_ge(s_dl, ONE + G * 2 + 2)
                    pe.wait_ge(s_pwl, ONE + G + 1)
                    pe.wait_ge(s_pl, ONE + (G + 1) * UNITS)
                    pe.wait_ge(s_pve, ONE + G * 2 + 2)
                    for jj, bank in enumerate((PT, R[2])):
                        for a in range(2):
                            w = slice(a * 256 + jj * P, a * 256 + (jj + 1) * P)
                            mm(bank[:, :], pw_h[:, w], d_h[:, a, :], start=(a == 0), stop=False)
                            mm(bank[:, :], pw_h[:, w], d_l[:, a, :], start=False, stop=False)
                            last = mm(bank[:, :], pw_l[:, w], d_h[:, a, :], start=False, stop=(a == 1))
                        last.then_inc(s_mix, 1)

                group(0, 0, True)
                group(1, 0, False)
                with pe.Fori(2, GROUPS) as g:
                    group(g, 1, False)

                def project(nb, frames):
                    pe.wait_ge(s_gt[2], ONE + (h + 1) * GROUPS)
                    pe.wait_ge(s_ex, ONE + (h + 1) * GROUPS * UNITS * (QUAD + 1))
                    for k in range(KT):
                        pe.wait_ge(s_ml, (h * OB + nb) * KT + k + 1)
                        pe.wait_ge(s_wl, ONE + h * NBLK + IN_BLKS + nb * KT + k + 1)
                        for r in range(ROWT):
                            if k == 0:
                                pe.wait_ge(s_ye, YB_FREE + (h * OB + nb) * ROWT - ROWT + r + 1)
                                if r == ROWT - 1:
                                    pe.wait_ge(s_oe, ONE + (h + 1) * GROUPS * UNITS)
                            c = slice(r * P, (r + 1) * P)
                            mh, ml = mix_h[k % 4][:, c], mix_l[k % 4][:, c]
                            mm(YB[r], mh, wh[:, k % SPLIT, :], start=(k == 0), stop=False)
                            mm(YB[r], mh, wl[:, k % SPLIT, :], start=False, stop=False)
                            last = mm(YB[r], ml, wh[:, k % SPLIT, :], start=False, stop=(k == KT - 1))
                            if k == KT - 1 and r < ROWT - 1:
                                last.then_inc(s_y, 1)
                        last.then_inc(s_blk, 1)
                        if frames is not None and X_AT[frames] <= k < X_AT[frames] + XG:
                            q = k - X_AT[frames]
                            if q == 0:
                                pe.wait_ge(s_xn, ROWT + 2 + nb)
                                pe.wait_ge(s_gt[3], ONE + (h + 1) * GROUPS)
                                pe.wait_ge(s_oe, ONE + (h + 1) * GROUPS * UNITS)
                                pe.wait_ge(s_me, ONE + (h + 1) * GROUPS * 2)
                            pe.wait_ge(s_xl, 1 + XG * (ROWT + nb - 1) + q + 1)
                            x_group(frames, q)

                if h == 0:
                    with pe.Fori(0, 2) as i:
                        for v in range(2):
                            project(i * 2 + v, v)
                else:
                    with pe.Fori(0, OB) as nb:
                        project(nb, None)



def _block_layout(w_in):
    import numpy as np
    tiles = [24, 25] + list(range(16, 24))
    for g in range(GROUPS):
        tiles += [26 + 2 * g, 27 + 2 * g, 2 * g, 2 * g + 1, 8 + 2 * g, 9 + 2 * g]
    w = w_in.reshape(4, 4, P, -1, P)
    w = w[:, :, :, tiles, :].transpose(3, 0, 2, 1, 4)
    return np.ascontiguousarray(w).reshape(len(tiles) * 4, P, BLK)


def _constants():
    import numpy as np
    c = np.zeros((P, C_N), np.float32)
    c[:, C_ID:C_ID + P] = np.eye(P)
    c[:, C_BLK:C_BLK + P] = np.kron(np.eye(2), np.ones((HD, HD)))
    c[:, C_MASK:C_MASK + CHUNK] = MASKED
    for g in range(GROUPS):
        c[:, C_INVW + g] = 0.5 ** (g + 1)
    c[:, C_EPS] = EPS
    return c


def kernel(x, meta_tokens, norm_g, w_in, pool_w, pool_scale, q_norm_g, k_norm_g, sinks, w_out):
    import numpy as np
    import concourse.bacc as bacc
    from concourse.bass_utils import run_bass_kernel_spmd

    a = lambda t: np.asarray(t)
    vecs = np.concatenate([
        a(pool_scale)[0].reshape(PAIRS, P).T,
        np.repeat(a(sinks)[0].reshape(PAIRS, 2).T, HD, axis=0),
        np.tile(a(q_norm_g)[0], 2)[:, None],
        np.tile(a(k_norm_g)[0], 2)[:, None],
        a(norm_g)[0].reshape(KT, P).T], axis=1)
    arrays = {
        "xcat": np.concatenate([a(meta_tokens), a(x)[0]], axis=0),
        "norm_g_in": a(norm_g)[0],
        "w_in_blocks": _block_layout(a(w_in)[0]),
        "w_out_in": a(w_out)[0],
        "pool_w_in": a(pool_w)[0],
        "vecs": vecs,
        "consts": _constants(),
    }
    arrays = {n: np.ascontiguousarray(v) for n, v in arrays.items()}
    nc = bacc.Bacc("TRN2", target_bir_lowering=False, num_devices=1)
    args = [nc.dram_tensor(n, v.shape, mybir.dt.from_np(v.dtype), kind="ExternalInput").ap()
            for n, v in arrays.items()]
    out = nc.dram_tensor("out", (SEQ, D), mybir.dt.float32, kind="ExternalOutput").ap()
    hymba_layer(nc, *args, out)
    got = run_bass_kernel_spmd(nc, [arrays], core_ids=[0]).results[0]["out"]
    return np.asarray(got).reshape(1, SEQ, D)
```
